# Optimizing a Trainium2 kernel written in Bass

```python
import math
import jax, jax.numpy as jnp
from jax import lax
import numpy as np

D_MODEL = 1024
BATCH = 1
SEQ = 512
DEPTH = 1

N_META = 16
BLOCK = 128
MLA_HEADS = 8
QK_NOPE = 64
QK_ROPE = 32
V_HEAD = 64
Q_LORA = 256
KV_LORA = 128
ROPE_THETA = 10000.0
MLA_WIDTH = MLA_HEADS * V_HEAD
CONV_CH = 512
CONV_K = 31
CONV_WIDTH = CONV_CH
MIX_WIDTH = MLA_WIDTH + CONV_WIDTH
IN_COLS = 2 * CONV_CH + Q_LORA + KV_LORA + QK_ROPE
N_KEYS = 128
N_EXPERTS = N_KEYS * N_KEYS
PEER_HEADS = 8
PEER_DK = 128
PEER_DK_HALF = PEER_DK // 2
PEER_TOPK = 16
PEER_CHUNK = 128
NORM_EPS = 1e-6


def rmsnorm(x, g):
    xf = x.astype(jnp.float32)
    y = xf * lax.rsqrt(jnp.mean(xf * xf, axis=-1, keepdims=True) + NORM_EPS)
    return (y * g.astype(jnp.float32)).astype(x.dtype)

def layernorm(x, g, b):
    xf = x.astype(jnp.float32)
    mu = jnp.mean(xf, axis=-1, keepdims=True)
    var = jnp.mean(jnp.square(xf - mu), axis=-1, keepdims=True)
    y = (xf - mu) * lax.rsqrt(var + NORM_EPS)
    return (y * g.astype(jnp.float32) + b.astype(jnp.float32)).astype(x.dtype)

def rope(x, pos):
    half = x.shape[-1] // 2
    freqs = ROPE_THETA ** (-jnp.arange(half, dtype=jnp.float32) / half)
    ang = pos.astype(jnp.float32)[:, None] * freqs[None, :]
    cos = jnp.cos(ang)[None, :, None, :].astype(x.dtype)
    sin = jnp.sin(ang)[None, :, None, :].astype(x.dtype)
    x1, x2 = x[..., :half], x[..., half:]
    return jnp.concatenate([x1 * cos - x2 * sin, x2 * cos + x1 * sin], axis=-1)

def causal_block_attention(q, k, v):
    B, Tp, H, Dq = q.shape
    nb = Tp // BLOCK
    qb = q.reshape(B, nb, BLOCK, H, Dq).transpose(1, 0, 2, 3, 4)
    kpos = jnp.arange(Tp)
    scale = 1.0 / math.sqrt(Dq)

    def one(args):
        qblk, i = args
        s = jnp.einsum('bqhd,bkhd->bhqk', qblk, k).astype(jnp.float32) * scale
        qpos = i * BLOCK + jnp.arange(BLOCK)
        mask = kpos[None, :] <= qpos[:, None]
        s = jnp.where(mask[None, None], s, -jnp.inf)
        p = jax.nn.softmax(s, axis=-1).astype(v.dtype)
        return jnp.einsum('bhqk,bkhd->bqhd', p, v)

    o = lax.map(one, (qb, jnp.arange(nb)))
    return o.transpose(1, 0, 2, 3, 4).reshape(B, Tp, H, v.shape[-1])

def mla_group(c_q, c_kv, k_rope_in, pos, g_q, w_uq, g_kv, w_ukv):
    B, Tp, _ = c_q.shape
    q = (rmsnorm(c_q, g_q) @ w_uq).reshape(B, Tp, MLA_HEADS, QK_NOPE + QK_ROPE)
    q = jnp.concatenate([q[..., :QK_NOPE], rope(q[..., QK_NOPE:], pos)], axis=-1)
    kv = (rmsnorm(c_kv, g_kv) @ w_ukv).reshape(B, Tp, MLA_HEADS, QK_NOPE + V_HEAD)
    k_nope, v = kv[..., :QK_NOPE], kv[..., QK_NOPE:]
    k_r = rope(k_rope_in[:, :, None, :], pos)
    k = jnp.concatenate([k_nope, jnp.broadcast_to(k_r, (B, Tp, MLA_HEADS, QK_ROPE))], axis=-1)
    o = causal_block_attention(q, k, v)
    return o.reshape(B, Tp, MLA_WIDTH)

def conv_group(a, b, conv_w, conv_b, g_ln, b_ln):
    h = a * jax.nn.sigmoid(b)
    h = lax.conv_general_dilated(h, conv_w[:, None, :].astype(h.dtype), window_strides=(1,),
                                 padding=[(CONV_K - 1, 0)],
                                 dimension_numbers=('NWC', 'WIO', 'NWC'),
                                 feature_group_count=CONV_CH) + conv_b
    h = layernorm(h, g_ln, b_ln)
    return jax.nn.silu(h)

def peer_ffn(xn, wq, keys, u_tab, v_tab):
    B, Tp, D = xn.shape
    xc = xn.reshape(-1, PEER_CHUNK, D)
    K = PEER_TOPK

    def one(xb):
        C = xb.shape[0]
        q = (xb @ wq).reshape(C, PEER_HEADS, 2, PEER_DK_HALF)
        s = jnp.einsum('chpd,hpnd->chpn', q, keys).astype(jnp.float32)
        sv, si = lax.top_k(s, K)
        cand = sv[:, :, 0, :, None] + sv[:, :, 1, None, :]
        cidx = si[:, :, 0, :, None] * N_KEYS + si[:, :, 1, None, :]
        top_s, sel = lax.top_k(cand.reshape(C, PEER_HEADS, K * K), K)
        eidx = jnp.take_along_axis(cidx.reshape(C, PEER_HEADS, K * K), sel, axis=-1)
        g = jax.nn.softmax(top_s, axis=-1)
        u = u_tab[eidx]
        act = jax.nn.gelu(jnp.einsum('chkd,cd->chk', u, xb).astype(jnp.float32), approximate=False)
        w = (g * act).astype(xb.dtype)
        return jnp.einsum('chk,chkd->cd', w, v_tab[eidx])

    return lax.map(one, xc).reshape(B, Tp, D)

def first_inputs(seed: int = 0) -> dict:
    key = jax.random.key(seed)
    ks = jax.random.split(key, 24)
    f32 = jnp.float32
    L, D = DEPTH, D_MODEL

    def nrm(k, shape, scale):
        return jax.random.normal(k, shape, f32) * scale

    def gain(k, shape):
        return 1.0 + 0.02 * jax.random.normal(k, shape, f32)

    return {
        "x": jax.random.normal(ks[0], (BATCH, SEQ, D), f32),
        "meta": nrm(ks[1], (N_META, D), 1.0),
        "g_mix_norm": gain(ks[2], (L, D)),
        "w_in": nrm(ks[3], (L, D, IN_COLS), D ** -0.5),
        "g_q": gain(ks[4], (L, Q_LORA)),
        "w_uq": nrm(ks[5], (L, Q_LORA, MLA_HEADS * (QK_NOPE + QK_ROPE)), Q_LORA ** -0.5),
        "g_kv": gain(ks[6], (L, KV_LORA)),
        "w_ukv": nrm(ks[7], (L, KV_LORA, MLA_HEADS * (QK_NOPE + V_HEAD)), KV_LORA ** -0.5),
        "conv_w": nrm(ks[8], (L, CONV_K, CONV_CH), CONV_K ** -0.5),
        "conv_b": nrm(ks[9], (L, CONV_CH), 0.02),
        "g_conv_ln": gain(ks[10], (L, CONV_CH)),
        "b_conv_ln": nrm(ks[11], (L, CONV_CH), 0.02),
        "g_out_attn": gain(ks[12], (L, MLA_WIDTH)),
        "g_out_conv": gain(ks[13], (L, CONV_WIDTH)),
        "w_out": nrm(ks[14], (L, MIX_WIDTH, D), MIX_WIDTH ** -0.5),
        "g_ffn_norm": gain(ks[15], (L, D)),
        "peer_wq": nrm(ks[16], (L, D, PEER_HEADS * PEER_DK), D ** -0.5),
        "peer_keys": nrm(ks[17], (L, PEER_HEADS, 2, N_KEYS, PEER_DK_HALF), PEER_DK_HALF ** -0.5),
        "peer_u": nrm(ks[18], (L, N_EXPERTS, D), D ** -0.5),
        "peer_v": nrm(ks[19], (L, N_EXPERTS, D), (PEER_HEADS * PEER_TOPK) ** -0.5),
        "g_final": gain(ks[20], (D,)),
    }

def first_block(x, meta, g_mix_norm, w_in, g_q, w_uq, g_kv, w_ukv, conv_w, conv_b, g_conv_ln, b_conv_ln,
              g_out_attn, g_out_conv, w_out, g_ffn_norm, peer_wq, peer_keys, peer_u, peer_v, g_final):
    B, S, D = x.shape
    T = N_META + S
    Tp = ((T + BLOCK - 1) // BLOCK) * BLOCK
    h = jnp.concatenate([jnp.broadcast_to(meta.astype(x.dtype)[None], (B, N_META, D)), x,
                         jnp.zeros((B, Tp - T, D), x.dtype)], axis=1)
    pos = jnp.arange(Tp, dtype=jnp.int32)

    c0 = 2 * CONV_CH
    c1 = c0 + Q_LORA
    c2 = c1 + KV_LORA
    for l in range(DEPTH):
        hn = rmsnorm(h, g_mix_norm[l])
        z = hn @ w_in[l]
        conv_out = conv_group(z[..., :CONV_CH], z[..., CONV_CH:c0], conv_w[l], conv_b[l],
                              g_conv_ln[l], b_conv_ln[l])
        attn_out = mla_group(z[..., c0:c1], z[..., c1:c2], z[..., c2:], pos,
                             g_q[l], w_uq[l], g_kv[l], w_ukv[l])
        mixed = jnp.concatenate([rmsnorm(attn_out, g_out_attn[l]),
                                 rmsnorm(conv_out, g_out_conv[l])], axis=-1)
        h = h + mixed @ w_out[l]
        h = h + peer_ffn(rmsnorm(h, g_ffn_norm[l]), peer_wq[l], peer_keys[l], peer_u[l], peer_v[l])

    h = rmsnorm(h, g_final)
    return h[:, N_META:N_META + S, :]


N_HEADS = 16
HEAD_DIM = 64
ATTN_WIDTH = N_HEADS * HEAD_DIM
KV_LATENT = 128
IDX_HEADS = 8
IDX_DIM = 64
TOPK_MAX = 256
Q_BLOCK = 128
RNN_WIDTH = 1024
RNN_BLOCKS = 16
RNN_BLOCK_DIM = RNN_WIDTH // RNN_BLOCKS
CONV_WIDTH_2 = 4
LRU_C = 8.0
SPLITS = (ATTN_WIDTH, KV_LATENT, IDX_HEADS * IDX_DIM, IDX_DIM, IDX_HEADS, ATTN_WIDTH, RNN_WIDTH, RNN_WIDTH, 2 * D_MODEL)
IN_WIDTH = sum(SPLITS)


def rms_norm(x, g):
    xf = x.astype(jnp.float32)
    y = xf * lax.rsqrt(jnp.mean(xf * xf, axis=-1, keepdims=True) + NORM_EPS)
    return (y * g.astype(jnp.float32)).astype(x.dtype)

def layer_norm(x, g, b):
    xf = x.astype(jnp.float32)
    mu = jnp.mean(xf, axis=-1, keepdims=True)
    xc = xf - mu
    y = xc * lax.rsqrt(jnp.mean(xc * xc, axis=-1, keepdims=True) + NORM_EPS)
    return (y * g.astype(jnp.float32) + b.astype(jnp.float32)).astype(x.dtype)

def alibi_slopes(n):
    return jnp.exp2(-8.0 * jnp.arange(1, n + 1, dtype=jnp.float32) / n)

def split_cols(z):
    offsets = np.cumsum(np.array(SPLITS))[:-1].tolist()
    return jnp.split(z, offsets, axis=-1)

def sparse_mla_attention(q, c_kv, q_idx, k_idx, w_idx, w_uk, w_uv):
    B, S = q.shape[0], q.shape[1]
    topk = min(TOPK_MAX, S // 4)
    tb = min(Q_BLOCK, S)
    nblk = S // tb
    f32 = jnp.float32
    q_lat = jnp.einsum('bshd,hcd->bshc', q, w_uk) * (HEAD_DIM ** -0.5)
    slopes = alibi_slopes(N_HEADS)
    key_pos = jnp.arange(S, dtype=jnp.int32)
    k_idx_f = k_idx.astype(f32)

    def to_blocks(a):
        return a.reshape((B, nblk, tb) + a.shape[2:]).swapaxes(0, 1)

    def block_fn(args):
        ql, qi, wi, t0 = args
        t = t0 + jnp.arange(tb, dtype=jnp.int32)
        s_idx = jax.nn.relu(jnp.einsum('btjd,bsd->btjs', qi.astype(f32), k_idx_f))
        s_idx = jnp.einsum('btjs,btj->bts', s_idx, wi.astype(f32))
        causal = key_pos[None, :] <= t[:, None]
        s_idx = jnp.where(causal[None], s_idx, -jnp.inf)
        _, idx = lax.top_k(s_idx, topk)
        c_sel = jax.vmap(lambda c, i: c[i])(c_kv, idx).astype(f32)
        logits = jnp.einsum('bthc,btkc->bthk', ql.astype(f32), c_sel)
        dist = (t[None, :, None] - idx).astype(f32)
        logits = logits - slopes[None, None, :, None] * dist[:, :, None, :]
        valid = idx <= t[None, :, None]
        logits = jnp.where(valid[:, :, None, :], logits, -jnp.inf)
        p = jax.nn.softmax(logits, axis=-1)
        o = jnp.einsum('bthk,btkc->bthc', p, c_sel)
        return o.astype(ql.dtype)

    t0s = jnp.arange(nblk, dtype=jnp.int32) * tb
    o_lat = lax.map(block_fn, (to_blocks(q_lat), to_blocks(q_idx), to_blocks(w_idx), t0s))
    o_lat = o_lat.swapaxes(0, 1).reshape(B, S, N_HEADS, KV_LATENT)
    return jnp.einsum('bshc,hcd->bshd', o_lat, w_uv)

def causal_depthwise_conv(x, w, b):
    S = x.shape[1]
    xp = jnp.pad(x, ((0, 0), (CONV_WIDTH_2 - 1, 0), (0, 0)))
    out = b
    for k in range(CONV_WIDTH_2):
        out = out + xp[:, k:k + S] * w[k]
    return out

def rg_lru(x, w_a, b_a, w_x, b_x, lam):
    B, S, C = x.shape
    f32 = jnp.float32
    xb = x.reshape(B, S, RNN_BLOCKS, RNN_BLOCK_DIM)
    r = jax.nn.sigmoid(jnp.einsum('bsgi,gij->bsgj', xb, w_a).reshape(B, S, C) + b_a).astype(f32)
    i = jax.nn.sigmoid(jnp.einsum('bsgi,gij->bsgj', xb, w_x).reshape(B, S, C) + b_x).astype(f32)
    log_a = -LRU_C * r * jax.nn.softplus(-lam.astype(f32))
    a = jnp.exp(log_a)
    b_in = jnp.sqrt(-jnp.expm1(2.0 * log_a)) * (i * x.astype(f32))

    def combine(left, right):
        a1, b1 = left
        a2, b2 = right
        return a1 * a2, a2 * b1 + b2

    _, h = lax.associative_scan(combine, (a, b_in), axis=1)
    return h.astype(x.dtype)

def hybrid_layer(x, norm_g, w_in, b_merge, kv_norm_g, w_uk, w_uv, idx_ln_g, idx_ln_b,
                 w_attn_proj, conv_w, conv_b, w_rg_a, b_rg_a, w_rg_x, b_rg_x, lru_lambda,
                 w_rnn_proj, w_out):
    B, S, _ = x.shape
    xn = rms_norm(x, norm_g)
    z = xn @ w_in
    q, c_kv, q_idx, k_idx, w_idx, g_attn, x_rnn, g_rnn, merge = split_cols(z)
    q = q.reshape(B, S, N_HEADS, HEAD_DIM)
    c_kv = rms_norm(c_kv, kv_norm_g)
    q_idx = q_idx.reshape(B, S, IDX_HEADS, IDX_DIM) * (IDX_DIM ** -0.5)
    k_idx = layer_norm(k_idx, idx_ln_g, idx_ln_b)
    w_idx = w_idx * (IDX_HEADS ** -0.5)
    o = sparse_mla_attention(q, c_kv, q_idx, k_idx, w_idx, w_uk, w_uv).reshape(B, S, ATTN_WIDTH)
    y_attn = (o * jax.nn.silu(g_attn)) @ w_attn_proj
    h = rg_lru(causal_depthwise_conv(x_rnn, conv_w, conv_b), w_rg_a, b_rg_a, w_rg_x, b_rg_x, lru_lambda)
    y_rnn = (h * jax.nn.silu(g_rnn)) @ w_rnn_proj
    gates = jax.nn.sigmoid(merge + b_merge)
    g_a, g_r = gates[..., :D_MODEL], gates[..., D_MODEL:]
    mixed = g_a * y_attn + g_r * y_rnn
    return x + mixed @ w_out

def second_inputs(seed: int = 0) -> dict:
    key = jax.random.key(seed)
    ks = jax.random.split(key, 24)
    f32 = jnp.float32

    def nrm(k, shape, scale):
        return jax.random.normal(k, shape, f32) * scale

    u = jax.random.uniform(ks[20], (DEPTH, RNN_WIDTH), f32, minval=0.9, maxval=0.999)
    return {
        'x': jax.random.normal(ks[0], (BATCH, SEQ, D_MODEL), f32),
        'norm_gain': 1.0 + nrm(ks[1], (DEPTH, D_MODEL), 0.01),
        'w_in': nrm(ks[2], (DEPTH, D_MODEL, IN_WIDTH), D_MODEL ** -0.5),
        'b_merge': nrm(ks[3], (DEPTH, 2 * D_MODEL), 0.01),
        'kv_norm_gain': 1.0 + nrm(ks[4], (DEPTH, KV_LATENT), 0.01),
        'w_uk': nrm(ks[5], (DEPTH, N_HEADS, KV_LATENT, HEAD_DIM), KV_LATENT ** -0.5),
        'w_uv': nrm(ks[6], (DEPTH, N_HEADS, KV_LATENT, HEAD_DIM), KV_LATENT ** -0.5),
        'idx_ln_gain': 1.0 + nrm(ks[7], (DEPTH, IDX_DIM), 0.01),
        'idx_ln_bias': nrm(ks[8], (DEPTH, IDX_DIM), 0.01),
        'w_attn_proj': nrm(ks[9], (DEPTH, ATTN_WIDTH, D_MODEL), ATTN_WIDTH ** -0.5),
        'conv_w': nrm(ks[10], (DEPTH, CONV_WIDTH_2, RNN_WIDTH), CONV_WIDTH_2 ** -0.5),
        'conv_b': nrm(ks[11], (DEPTH, RNN_WIDTH), 0.01),
        'w_rg_a': nrm(ks[12], (DEPTH, RNN_BLOCKS, RNN_BLOCK_DIM, RNN_BLOCK_DIM), RNN_BLOCK_DIM ** -0.5),
        'b_rg_a': nrm(ks[13], (DEPTH, RNN_WIDTH), 0.01),
        'w_rg_x': nrm(ks[14], (DEPTH, RNN_BLOCKS, RNN_BLOCK_DIM, RNN_BLOCK_DIM), RNN_BLOCK_DIM ** -0.5),
        'b_rg_x': nrm(ks[15], (DEPTH, RNN_WIDTH), 0.01),
        'lru_lambda': jnp.log(u) - jnp.log1p(-u),
        'w_rnn_proj': nrm(ks[16], (DEPTH, RNN_WIDTH, D_MODEL), RNN_WIDTH ** -0.5),
        'w_out': nrm(ks[17], (DEPTH, D_MODEL, D_MODEL), D_MODEL ** -0.5),
        'final_norm_gain': 1.0 + nrm(ks[18], (D_MODEL,), 0.01),
    }

def second_block(x, norm_gain, w_in, b_merge, kv_norm_gain, w_uk, w_uv, idx_ln_gain, idx_ln_bias,
              w_attn_proj, conv_w, conv_b, w_rg_a, b_rg_a, w_rg_x, b_rg_x, lru_lambda,
              w_rnn_proj, w_out, final_norm_gain):
    for l in range(DEPTH):
        x = hybrid_layer(x, norm_gain[l], w_in[l], b_merge[l], kv_norm_gain[l], w_uk[l], w_uv[l],
                         idx_ln_gain[l], idx_ln_bias[l], w_attn_proj[l], conv_w[l], conv_b[l],
                         w_rg_a[l], b_rg_a[l], w_rg_x[l], b_rg_x[l], lru_lambda[l],
                         w_rnn_proj[l], w_out[l])
    return rms_norm(x, final_norm_gain)


def setup_inputs(seed=0):
    out = dict(first_inputs(seed))
    for name, value in second_inputs(seed + 1).items():
        if name != "x":
            out[name + "_2"] = value
    return out


def reference(
    x, meta, g_mix_norm, w_in, g_q, w_uq, g_kv, w_ukv, conv_w, conv_b, g_conv_ln, b_conv_ln,
    g_out_attn, g_out_conv, w_out, g_ffn_norm, peer_wq, peer_keys, peer_u, peer_v, g_final,
    norm_gain_2, w_in_2, b_merge_2, kv_norm_gain_2, w_uk_2, w_uv_2, idx_ln_gain_2,
    idx_ln_bias_2, w_attn_proj_2, conv_w_2, conv_b_2, w_rg_a_2, b_rg_a_2, w_rg_x_2, b_rg_x_2,
    lru_lambda_2, w_rnn_proj_2, w_out_2, final_norm_gain_2,
):
    x = first_block(
        x, meta, g_mix_norm, w_in, g_q, w_uq, g_kv, w_ukv, conv_w, conv_b, g_conv_ln, b_conv_ln,
        g_out_attn, g_out_conv, w_out, g_ffn_norm, peer_wq, peer_keys, peer_u, peer_v, g_final,
    )
    return second_block(
        x, norm_gain_2, w_in_2, b_merge_2, kv_norm_gain_2, w_uk_2, w_uv_2, idx_ln_gain_2,
        idx_ln_bias_2, w_attn_proj_2, conv_w_2, conv_b_2, w_rg_a_2, b_rg_a_2, w_rg_x_2,
        b_rg_x_2, lru_lambda_2, w_rnn_proj_2, w_out_2, final_norm_gain_2,
    )


_drawn_inputs = setup_inputs


def setup_inputs(seed=0):
    import zlib

    import numpy as np

    out = dict(_drawn_inputs(seed))
    spreads = {}
    factors = {'g_q': 3.404,
     'g_conv_ln': 2.803,
     'b_conv_ln': 3.157,
     'g_out_attn': 3.22,
     'g_out_conv': 3.092,
     'g_ffn_norm': 5.393,
     'norm_gain_2': 3.874,
     'b_merge_2': 28.15,
     'kv_norm_gain_2': 8.0,
     'idx_ln_gain_2': 5.772,
     'idx_ln_bias_2': 6.702,
     'conv_b_2': 7.345,
     'b_rg_a_2': 64.0,
     'b_rg_x_2': 64.0,
     'final_norm_gain_2': 31.141}
    for name, (base, spread) in spreads.items():
        noise = np.random.default_rng([zlib.crc32(name.encode()), seed]).standard_normal(out[name].shape)
        drawn = base * np.exp(spread * noise) if base else spread * noise
        out[name] = __import__('jax').numpy.asarray(drawn.astype(out[name].dtype))
    for name, factor in factors.items():
        out[name] = (out[name] * factor).astype(out[name].dtype)
    return out
```

```python
from contextlib import ExitStack

import numpy as np

import concourse.bass as bass
from concourse import mybir

F32 = mybir.dt.float32
F32R = mybir.dt.float32r
BF16 = mybir.dt.bfloat16
U32 = mybir.dt.uint32
ALU = mybir.AluOpType
ACT = mybir.ActivationFunctionType
AX = mybir.AxisListType

D = 1024
META = 16
S = 512
T = META + S
KT = D // 128
EPS = 1e-6
BIG = 1e30
TAKEN = -3e38

GAINS = [
    ("g_mix", 8), ("g_q", 2), ("g_kv", 1), ("conv_w", 4 * 31), ("conv_b", 4), ("g_ln", 4), ("b_ln", 4),
    ("g_oa", 4), ("g_oc", 4), ("g_ffn", 8), ("g_fin", 8), ("g2", 8), ("b_merge", 16), ("g_kv2", 1),
    ("g_idx", 1), ("b_idx", 1), ("conv_w2", 8 * 4), ("conv_b2", 8), ("b_a", 8), ("b_x", 8), ("lam", 8),
    ("g_fin2", 8),
]
GCOL = {}
NG = 0
for _name, _n in GAINS:
    GCOL[_name] = NG
    NG += _n

N_GROUPS = 16
N_TILES = 12 + 8 + 8 + 128 + 128 + 54 + 8 * 3


class Engine:

    def __init__(self, sem):
        self.sem = sem
        self.count = 0
        self.queue = []
        self.reached = {}

    def wait(self, *tokens):
        for token in tokens:
            if token is None:
                continue
            sem, value = token
            if self.reached.get(sem, 0) < value:
                self.reached[sem] = value
                self.queue.append(lambda e, s=sem, v=value: e.wait_ge(s, v))

    def op(self, fn, *tokens):
        self.wait(*tokens)
        self.count += 1
        self.queue.append(lambda e: fn(e).then_inc(self.sem, 1))
        return (self.sem, self.count)

    def silent(self, fn, *tokens):
        self.wait(*tokens)
        self.queue.append(fn)

    def last(self):
        return (self.sem, self.count) if self.count else None


class Channel:

    def __init__(self, sem):
        self.sem = sem
        self.count = 0

    def start(self, engine, out, in_, *tokens):
        engine.wait(*tokens)
        self.count += 16
        engine.queue.append(lambda e: e.dma_start(out, in_).then_inc(self.sem, 16))
        return (self.sem, self.count)

    def last(self):
        return (self.sem, self.count)


class Buf:

    def __init__(self, t):
        self.t = t
        self.free = []


class Ring:
    def __init__(self, bufs):
        self.bufs = bufs
        self.at = 0

    def next(self):
        b = self.bufs[self.at % len(self.bufs)]
        self.at += 1
        return b


def build_program(nc, hT, wstream, gains, consts, trig, w_uq, w_ukv, keys, w_uk, w_uv, w_rg, out, dbg=None):
    gdram = nc.dram_tensor("g_scratch", (128, 16, 128, 32), F32, kind="Internal").ap()
    ctx = ExitStack()
    with ctx:
        def sem(name):
            return ctx.enter_context(nc.semaphore(name))

        def sb(stack, name, shape, dt=F32):
            return stack.enter_context(nc.sbuf_tensor(name, shape, dt))

        pe = Engine(sem("s_pe"))
        dve = Engine(sem("s_dve"))
        act = Engine(sem("s_act"))
        pool = Engine(sem("s_pool"))
        sp = Engine(sem("s_sp"))
        engines = [pe, dve, act, pool]

        def channel(name):
            return Channel(sem(name))

        def fence(*more):
            tokens = [e.last() for e in engines] + list(more)
            for e in engines + [sp]:
                e.wait(*tokens)

        banks = [Buf(ctx.enter_context(nc.psum_tensor(f"bank{i}", [128, 512], F32))) for i in range(4)]
        wide = [Buf(ctx.enter_context(nc.psum_tensor(f"wide{i}", [128, 1024], F32))) for i in range(2)]
        gemm_banks = Ring(banks)
        wide_banks = Ring(wide)

        h = sb(ctx, "h", [128, KT, T])
        XH = sb(ctx, "XH", [128, KT, T], F32R)
        XL = sb(ctx, "XL", [128, KT, T], F32R)
        NRAW, NSPLIT = 4, 3
        wraw = [sb(ctx, f"wraw{i}", [128, 1024]) for i in range(NRAW)]
        wh = [sb(ctx, f"wh{i}", [128, 1024], F32R) for i in range(NSPLIT)]
        wl = [sb(ctx, f"wl{i}", [128, 1024], F32R) for i in range(NSPLIT)]
        gn = sb(ctx, "gn", [128, NG])
        cst = sb(ctx, "cst", [128, 1024])
        ident = cst[:, 0:128]
        cmask = cst[:, 128:256]
        iota = cst[:, 256:384]
        dist = cst[:, 384:896]
        ones = cst[:, 896:1024]
        identb = sb(ctx, "identb", [128, 128], BF16)
        cmaskb = sb(ctx, "cmaskb", [128, 128], BF16)
        st = sb(ctx, "st", [128, 3, 8])
        diag = sb(ctx, "diag", [128, 5, 128])
        rb = sb(ctx, "rb", [128, T])
        inv512 = sb(ctx, "inv512", [128, 128])
        inv64 = sb(ctx, "inv64", [128, 128])
        st_free = [None]
        rb_free = [None]

        def g(name, i=0):
            c = GCOL[name] + i
            return gn[:, c:c + 1]

        c_h = [channel(f"c_h{i}") for i in range(KT)]
        c_gn, c_cst = channel("c_gn"), channel("c_cst")
        t_gn = c_gn.start(sp, gn[:, :], gains)
        t_h = [c_h[k].start(sp, h[:, k, :], hT[:, k, :]) for k in range(KT)]
        t_cst = c_cst.start(sp, cst[:, :], consts)
        for e in engines:
            e.wait(t_cst, t_gn)
        t_b = [act.op(lambda e: e.copy(identb[:, :], ident)), act.op(lambda e: e.copy(cmaskb[:, :], cmask))]
        t_b += [act.op(lambda e: e.mul(inv512[:, :], ones, 1.0 / 512.0)),
                act.op(lambda e: e.mul(inv64[:, :], ones, 1.0 / 64.0))]
        pe.wait(*t_b)

        c_w = [channel(f"c_w{i}") for i in range(NRAW)]

        class Stream:
            loaded = 0
            split = 0
            used = 0
            raw_free = [[] for _ in range(NRAW)]
            raw_ready = {}
            parts_free = [[] for _ in range(NSPLIT)]
            ready = {}

            def load(self):
                n = self.loaded
                s = n % NRAW
                self.raw_ready[n] = c_w[s].start(sp, wraw[s][:, :], wstream[n], *self.raw_free[s])
                self.loaded += 1

            def part(self):
                n = self.split
                while self.loaded <= n:
                    self.load()
                r, s = n % NRAW, n % NSPLIT
                t1 = act.op(lambda e: e.copy(wh[s][:, :], wraw[r][:, :]), self.raw_ready[n], *self.parts_free[s])
                t2 = pool.op(lambda e: e.tensor_tensor(wl[s][:, :], wraw[r][:, :], wh[s][:, :].bitcast(F32),
                                                       ALU.subtract), t1, *self.parts_free[s])
                self.raw_free[r] = [t1, t2]
                self.ready[n] = (t1, t2)
                self.split += 1
                if self.loaded < min(n + NRAW, N_TILES):
                    self.load()

            def get(self):
                n = self.used
                while self.split < min(n + NSPLIT, N_TILES):
                    self.part()
                return n % NSPLIT, self.ready.pop(n)

            def done(self, token):
                self.parts_free[self.used % NSPLIT] = [token]
                self.used += 1

        ws = Stream()

        def gemm(xh, xl, chunks, x_ready):
            s, ready = ws.get()
            pe.wait(*ready)
            bs = [gemm_banks.next() for _ in chunks]
            toks = []
            for (a, b), bank in zip(chunks, bs):
                pe.wait(*bank.free)
                for k in range(KT):
                    pe.wait(*x_ready[k])
                    w1, w2 = wh[s][:, k * 128:k * 128 + 128], wl[s][:, k * 128:k * 128 + 128]
                    o = bank.t[:, 0:b - a]
                    x1, x2 = xh[:, k, a:b], xl[:, k, a:b]
                    pe.silent(lambda e, o=o, w=w1, x=x1, k=k: e.matmul(o, w, x, start=(k == 0), stop=False))
                    pe.silent(lambda e, o=o, w=w1, x=x2: e.matmul(o, w, x, start=False, stop=False))
                    f = lambda e, o=o, w=w2, x=x1, k=k: e.matmul(o, w, x, start=False, stop=(k == KT - 1))
                    if k == KT - 1:
                        toks.append(pe.op(f))
                    else:
                        pe.silent(f)
            ws.done(toks[-1])
            return bs, toks

        def mm_group(parts, *tokens):
            pe.wait(*tokens)
            for i, (o, l, r) in enumerate(parts):
                f = lambda e, o=o, l=l, r=r, i=i: e.matmul(o, l, r, start=(i == 0), stop=(i == len(parts) - 1))
                if i < len(parts) - 1:
                    pe.silent(f)
            return pe.op(f)

        def token_tiles(n):
            return [(t, min(128, n - t)) for t in range(0, n, 128)]

        def rms_scale(srcs, toks, n, size, sq, rows=128):
            tts = token_tiles(n)
            bank = gemm_banks.next()
            pe.wait(*bank.free)
            for k, src in enumerate(srcs):
                q = sq.next()
                t = act.op(lambda e, q=q, src=src: e.activation(q.t[0:rows, 0:n], src, ACT.Square), toks[k], *q.free)
                pe.wait(t)
                for j, (a, m) in enumerate(tts):
                    f = lambda e, q=q, j=j, a=a, m=m, k=k: e.matmul(
                        bank.t[0:m, j:j + 1], q.t[0:rows, a:a + m], ones[0:rows, 0:1], start=(k == 0 and j == 0),
                        stop=(k == len(srcs) - 1), skip_group_check=True)
                    if j < len(tts) - 1:
                        pe.silent(f)
                t_mm = pe.op(f)
                q.free = [t_mm]
            full = [(j, m) for j, (a, m) in enumerate(tts) if m == 128]
            parts = [(128, 0, len(full))] + [(m, j, j + 1) for j, (a, m) in enumerate(tts) if m < 128]
            dve.wait(st_free[0])
            ts = [dve.op(lambda e, p=p: e.tensor_scalar(st[0:p[0], 0, p[1]:p[2]], bank.t[0:p[0], p[1]:p[2]],
                                                        1.0 / size, EPS, ALU.mult, ALU.add), t_mm) for p in parts]
            bank.free = [ts[-1]]
            ts = [act.op(lambda e, p=p: e.sqrt(st[0:p[0], 1, p[1]:p[2]], st[0:p[0], 0, p[1]:p[2]]), ts[-1])
                  for p in parts]
            ts = [dve.op(lambda e, p=p: e.reciprocal(st[0:p[0], 2, p[1]:p[2]], st[0:p[0], 1, p[1]:p[2]]), ts[-1])
                  for p in parts]
            td = []
            for j, (a, m) in enumerate(tts):
                td.append(dve.op(lambda e, j=j, m=m: e.tensor_scalar(diag[0:m, j, 0:m], ident[0:m, 0:m],
                                                                     st[0:m, 2, j:j + 1], None, ALU.mult), ts[-1]))
            st_free[0] = td[-1]
            b2 = wide_banks.next()
            pe.wait(*b2.free)
            for j, (a, m) in enumerate(tts):
                t_bc = pe.op(lambda e, j=j, a=a, m=m: e.matmul(b2.t[:, a:a + m], ones[0:m, :], diag[0:m, j, 0:m],
                                                               start=True, stop=True), td[j])
            st_free[0] = t_bc
            t_rb = act.op(lambda e: e.copy(rb[:, 0:n], b2.t[:, 0:n]), t_bc, rb_free[0])
            b2.free = [t_rb]
            return t_rb

        def split(src, src_tok, xh, xl, *free):
            t1 = act.op(lambda e: e.copy(xh, src), src_tok, *free)
            t2 = pool.op(lambda e: e.tensor_tensor(xl, src, xh.bitcast(F32), ALU.subtract), t1, src_tok, *free)
            return (t1, t2)

        def scaled_split(src, gain, n, t_rb, tmp, xh, xl, *tokens):
            b = tmp.next()
            t = dve.op(lambda e: e.scalar_tensor_tensor(b.t[:, 0:n], src, gain, rb[:, 0:n], ALU.mult, ALU.mult),
                       t_rb, *b.free, *tokens)
            r = split(b.t[:, 0:n], t, xh, xl)
            b.free = list(r)
            rb_free[0] = t
            return r

        def dump(name, ap, *tokens):
            if dbg is not None and name in dbg:
                c = channel("c_dbg_" + name)
                t = c.start(sp, dbg[name], ap, *[e.last() for e in engines], *tokens)
                for e in engines:
                    e.wait(t)

        A = ExitStack()
        c_a = [channel(f"c_a{i}") for i in range(3)]
        tmp = Ring([Buf(sb(A, f"tmp{i}", [128, T])) for i in range(3)])
        sq = Ring([Buf(sb(A, f"sq{i}", [128, T])) for i in range(2)])
        trg = sb(A, "trg", [128, T])
        uq = sb(A, "uq", [128, 2048])
        ukv = sb(A, "ukv", [128, 1024])
        t_trg = c_a[0].start(sp, trg[:, :], trig)
        t_uq = c_a[1].start(sp, uq[:, :], w_uq)
        t_ukv = c_a[2].start(sp, ukv[:, :], w_ukv)
        cq = sb(A, "cq", [128, 3, T])
        cqn = sb(A, "cqn", [128, 3, T])
        kr = sb(A, "kr", [128, T])
        PADC = 14
        hc = sb(A, "hc", [128, 4, PADC + T])
        vt = sb(A, "vt", [128, 5, 512])
        kTh = Ring([Buf(sb(A, f"kTh{i}", [128, T])) for i in range(2)])
        qTh = Ring([Buf(sb(A, f"qTh{i}", [128, 512])) for i in range(2)])
        Pb = Ring([Buf(sb(A, f"P{i}", [128, T])) for i in range(3)])
        PTb = Ring([Buf(sb(A, f"PT{i}", [128, 5, 512])) for i in range(1)])
        mx = Ring([Buf(sb(A, f"mx{i}", [128, 4])) for i in range(6)])
        attn = sb(A, "attn", [128, 4, 512])
        co = sb(A, "co", [128, 4, 512])

        t_z = pool.op(lambda e: e.memset(hc[:, :, 0:PADC], 0.0))

        CH = [(0, 264), (264, 528)]
        t_rb = rms_scale([h[:, k, :] for k in range(KT)], t_h, T, D, sq)
        x_ready = [scaled_split(h[:, k, :], g("g_mix", k), T, t_rb, tmp, XH[:, k, :], XL[:, k, :]) for k in range(KT)]

        t_c = []
        for i in range(3):
            bs, tk = gemm(XH, XL, CH, x_ready)
            for (a, b), bank, t in zip(CH, bs, tk):
                te = act.op(lambda e, i=i, a=a, b=b, bank=bank: e.copy(cq[:, i, a:b], bank.t[:, 0:b - a]), t)
                bank.free = [te]
            t_c.append(te)
        bs, tk = gemm(XH, XL, CH, x_ready)
        dve.wait(t_trg)
        for (a, b), bank, t in zip(CH, bs, tk):
            u = tmp.next()
            t1 = dve.op(lambda e, a=a, b=b, bank=bank: e.tensor_tensor(kr[64:96, a:b], bank.t[64:96, 0:b - a],
                                                                       trg[64:96, a:b], ALU.mult), t)
            t2 = dve.op(lambda e, a=a, b=b, bank=bank, u=u: e.tensor_tensor(u.t[64:96, a:b], bank.t[96:128, 0:b - a],
                                                                            trg[96:128, a:b], ALU.mult), t, *u.free)
            bank.free = [t2]
            t_kr = dve.op(lambda e, a=a, b=b, u=u: e.tensor_tensor(kr[64:96, a:b], kr[64:96, a:b], u.t[64:96, a:b],
                                                                   ALU.add), t1, t2)
            u.free = [t_kr]
        t_hc = []
        for c in range(4):
            bsa, ta = gemm(XH, XL, CH, x_ready)
            bsb, tb = gemm(XH, XL, CH, x_ready)
            u = tmp.next()
            for i, (a, b) in enumerate(CH):
                ts = act.op(lambda e, a=a, b=b, u=u, bank=bsb[i]: e.activation(u.t[:, a:b], bank.t[:, 0:b - a],
                                                                               ACT.Sigmoid), tb[i], *u.free)
                bsb[i].free = [ts]
                tm = dve.op(lambda e, a=a, b=b, u=u, c=c, bank=bsa[i]: e.tensor_tensor(
                    hc[:, c, PADC + a:PADC + b], bank.t[:, 0:b - a], u.t[:, a:b], ALU.mult), ts, ta[i])
                bsa[i].free = [tm]
            u.free = [tm]
            t_hc.append(tm)
        dump("hc", hc[:, :, PADC:])

        t_rb = rms_scale([cq[:, 0, :], cq[:, 1, :]], [t_c[0], t_c[1]], T, 256, sq)
        t_qn = [dve.op(lambda e, i=i: e.scalar_tensor_tensor(cqn[:, i, :], cq[:, i, :], g("g_q", i), rb[:, :],
                                                             ALU.mult, ALU.mult), t_rb) for i in range(2)]
        rb_free[0] = t_qn[1]
        t_rb = rms_scale([cq[:, 2, :]], [t_c[2]], T, 128, sq)
        t_kvn = dve.op(lambda e: e.scalar_tensor_tensor(cqn[:, 2, :], cq[:, 2, :], g("g_kv"), rb[:, :],
                                                        ALU.mult, ALU.mult), t_rb)
        rb_free[0] = t_kvn

        pe.wait(t_uq, t_ukv)
        ktoks = [(0, META)] + [(META + 128 * i, 128) for i in range(4)]
        ukv_v = ukv[:, :].rearrange("p (h e) -> p h e", h=8)[:, :, 64:128]
        for i, (a, m) in enumerate(ktoks):
            bank = gemm_banks.next()
            t = mm_group([(bank.t[0:m, :], cqn[:, 2, a:a + m], ukv_v)], t_kvn, *bank.free)
            t_v = act.op(lambda e, i=i, m=m, bank=bank: e.copy(vt[0:m, i, :], bank.t[0:m, :]), t)
            bank.free = [t_v]

        taps = []
        t_co = [None] * 4

        def tap(c, k):
            w = g("conv_w", c * 31 + k)
            x = hc[:, c, k:k + 512]
            if k == 0:
                t_co[c] = dve.op(lambda e: e.tensor_scalar(co[:, c, :], x, w, g("conv_b", c), ALU.mult, ALU.add),
                                 t_hc[c], t_z)
            else:
                t_co[c] = dve.op(lambda e: e.scalar_tensor_tensor(co[:, c, :], x, w, co[:, c, :], ALU.mult, ALU.add),
                                 t_co[c])

        for k in range(31):
            for c in range(4):
                taps.append((c, k))

        def conv_some(n):
            for _ in range(min(n, len(taps))):
                tap(*taps.pop(0))

        SC = 1.0 / (96.0 ** 0.5)
        att_banks = Ring(banks[0:3])
        for hd in range(8):
            qb = qTh.next()
            bank = att_banks.next()
            t = mm_group([(bank.t[:, :], uq[:, hd * 256 + k * 128:hd * 256 + k * 128 + 128], cqn[:, k, META:T])
                          for k in range(2)], *t_qn, *bank.free)
            u, v = tmp.next(), tmp.next()
            dve.wait(*qb.free)
            t0 = act.op(lambda e, qb=qb, bank=bank: e.mul(qb.t[0:64, :], bank.t[0:64, :], SC), t, *qb.free)
            t1 = dve.op(lambda e, bank=bank, u=u: e.scalar_tensor_tensor(
                u.t[64:96, 0:512], bank.t[64:96, :], SC, trg[64:96, META:T], ALU.mult, ALU.mult), t0, *u.free)
            t2 = dve.op(lambda e, bank=bank, v=v: e.scalar_tensor_tensor(
                v.t[64:96, 0:512], bank.t[96:128, :], SC, trg[96:128, META:T], ALU.mult, ALU.mult), t, *v.free)
            t3 = dve.op(lambda e, qb=qb, u=u, v=v: e.tensor_tensor(qb.t[64:96, :], u.t[64:96, 0:512],
                                                                   v.t[64:96, 0:512], ALU.add), t1, t2)
            bank.free = [t0, t2]
            u.free = [t3]
            v.free = [t3]
            kb = kTh.next()
            wb = wide_banks.next()
            pe.wait(*wb.free, t_kvn)
            for a, b in ((0, 512), (512, T)):
                tk_ = pe.op(lambda e, a=a, b=b, wb=wb, hd=hd: e.matmul(wb.t[0:64, a:b], ukv[:, hd * 128:hd * 128 + 64],
                                                                       cqn[:, 2, a:b], start=True, stop=True))
            t4 = act.op(lambda e, kb=kb, wb=wb: e.copy(kb.t[0:64, :], wb.t[0:64, 0:T]), tk_, *kb.free)
            wb.free = [t4]
            t5 = dve.op(lambda e, kb=kb: e.tensor_copy(kb.t[64:96, :], kr[64:96, :]), t_kr, *kb.free)
            pt = PTb.next()
            pt_w = []
            for qt in range(4):
                n = META + 128 * (qt + 1)
                wb = wide_banks.next()
                pe.wait(*wb.free, t0, t3, t4, t5)
                d0 = META + 128 * qt
                regions = [(0, min(n, 512))] + ([(512, n)] if n > 512 else [])
                for a, b in regions:
                    pe.silent(lambda e, a=a, b=b, wb=wb, qb=qb, kb=kb, qt=qt: e.matmul(
                        wb.t[:, a:b], qb.t[0:96, qt * 128:qt * 128 + 128], kb.t[0:96, a:b], start=True, stop=False,
                        skip_group_check=True))
                    da, db = max(a, d0), min(b, n)
                    tS = pe.op(lambda e, da=da, db=db, wb=wb, d0=d0: e.matmul(
                        wb.t[:, da:db], identb[:, :], cmaskb[:, da - d0:db - d0], start=False, stop=True,
                        skip_group_check=True))
                m = mx.next()
                P = Pb.next()
                t6 = dve.op(lambda e, m=m, wb=wb, n=n: e.tensor_reduce(m.t[:, 0:1], wb.t[:, 0:n], AX.X, ALU.max,
                                                                       negate=True), tS, *m.free)
                t7 = act.op(lambda e, m=m, wb=wb, n=n, P=P: e.activation(
                    P.t[:, 0:n], wb.t[:, 0:n], ACT.Exp, bias=m.t[:, 0:1], accum_out=m.t[:, 1:2]), t6, *P.free)
                wb.free = [t7]
                t8 = dve.op(lambda e, m=m: e.reciprocal(m.t[:, 2:3], m.t[:, 1:2]), t7)
                t9 = dve.op(lambda e, m=m, P=P, n=n: e.tensor_scalar(P.t[:, 0:n], P.t[:, 0:n], m.t[:, 2:3], None,
                                                                     ALU.mult), t8)
                m.free = [t9]
                wb = wide_banks.next()
                pe.wait(t9, *wb.free)
                pe.silent(lambda e, wb=wb, P=P: e.transpose(wb.t[0:META, 512:640], P.t[:, 0:META], ident))
                for i in range(qt + 1):
                    f = lambda e, wb=wb, P=P, i=i: e.transpose(
                        wb.t[:, i * 128:i * 128 + 128], P.t[:, META + i * 128:META + i * 128 + 128], ident)
                    if i < qt:
                        pe.silent(f)
                tT = pe.op(f)
                P.free = [tT]
                ta_ = act.op(lambda e, wb=wb, pt=pt, qt=qt: e.copy(pt.t[0:META, 0, qt * 128:qt * 128 + 128],
                                                                   wb.t[0:META, 512:640]), tT, *pt.free)
                tb_ = dve.op(lambda e, wb=wb, pt=pt, qt=qt: e.tensor_copy(
                    pt.t[:, 1:qt + 2, qt * 128:qt * 128 + 128],
                    wb.t[:, 0:(qt + 1) * 128].rearrange("p (k q) -> p k q", q=128)), tT, *pt.free)
                wb.free = [ta_, tb_]
                pt_w += [ta_, tb_]
                conv_some(4)
            if hd % 2 == 0:
                pair = banks[3]
            b0 = 64 * (hd % 2)
            pe.wait(*pair.free, *pt_w, t_v)
            for i in range(5):
                mrows = META if i == 0 else 128
                q0 = 0 if i == 0 else 128 * (i - 1)
                f = lambda e, i=i, mrows=mrows, q0=q0, pair=pair, pt=pt, hd=hd, b0=b0: e.matmul(
                    pair.t[b0:b0 + 64, q0:512], vt[0:mrows, i, hd * 64:hd * 64 + 64], pt.t[0:mrows, i, q0:512],
                    start=(i == 0), stop=(i == 4), skip_group_check=True)
                if i < 4:
                    pe.silent(f)
            tO = pe.op(f)
            pt.free = [tO]
            qb.free = [tO]
            kb.free = [tO]
            if hd % 2 == 1:
                t_at = act.op(lambda e, pair=pair, hd=hd: e.copy(attn[:, hd // 2, :], pair.t[:, :]), tO)
                pair.free = [t_at]
        conv_some(200)
        dump("attn", attn[:, :, :])
        dump("co", co[:, :, :])

        t_rb = rms_scale([attn[:, i, :] for i in range(4)], [t_at] * 4, 512, 512, sq)
        mix_ready = [scaled_split(attn[:, i, :], g("g_oa", i), 512, t_rb, tmp, XH[:, i, 0:512], XL[:, i, 0:512],
                                  pe.last()) for i in range(4)]

        def layer_mean(srcs, toks, inv, rows=128):
            bank = gemm_banks.next()
            b = mm_group([(bank.t[:, :], inv, s) for s in srcs], *toks, *bank.free)
            return bank, b

        bank, t = layer_mean([co[:, c, :] for c in range(4)], t_co, inv512[:, :])
        for c in range(4):
            t_co[c] = dve.op(lambda e, c=c, bank=bank: e.tensor_tensor(co[:, c, :], co[:, c, :], bank.t[:, :],
                                                                       ALU.subtract), t)
        bank.free = [t_co[3]]
        t_rb = rms_scale([co[:, c, :] for c in range(4)], t_co, 512, 512, sq)
        t_silu = []
        for c in range(4):
            t1 = dve.op(lambda e, c=c: e.scalar_tensor_tensor(co[:, c, :], co[:, c, :], g("g_ln", c), rb[:, 0:512],
                                                              ALU.mult, ALU.mult), t_rb)
            rb_free[0] = t1
            t_silu.append(act.op(lambda e, c=c: e.activation(co[:, c, :], co[:, c, :], ACT.Silu, bias=g("b_ln", c)),
                                 t1))
        t_rb = rms_scale([co[:, c, :] for c in range(4)], t_silu, 512, 512, sq)
        mix_ready += [scaled_split(co[:, c, :], g("g_oc", c), 512, t_rb, tmp, XH[:, 4 + c, 0:512], XL[:, 4 + c, 0:512])
                      for c in range(4)]
        FULL = [(0, 512)]
        t_hk = []
        for m in range(8):
            (bank,), (t,) = gemm(XH, XL, FULL, mix_ready)
            tt = dve.op(lambda e, m=m, bank=bank: e.tensor_tensor(h[:, m, META:T], bank.t[:, :], h[:, m, META:T],
                                                                  ALU.add), t)
            bank.free = [tt]
            t_hk.append(tt)
        dump("h1", h[:, :, META:])
        fence()
        A.close()

        B = ExitStack()
        c_b = channel("c_b")
        tmp = Ring([Buf(sb(B, f"btmp{i}", [128, 512])) for i in range(3)])
        sq = Ring([Buf(sb(B, f"bsq{i}", [128, 512])) for i in range(2)])
        ky = sb(B, "ky", [128, 8, 128])
        t_ky = c_b.start(sp, ky[:, :, :], keys)
        qp = sb(B, "qp", [128, 8, 512])
        sv = sb(B, "sv", [128, 16, 16])
        siu = sb(B, "siu", [128, 16, 16], U32)
        sif = sb(B, "sif", [128, 16, 16])
        left = sb(B, "left", [128, 8, 128])
        cand = sb(B, "cand", [128, 8, 256])
        left2 = sb(B, "left2", [128, 8, 256])
        hot = left2[:, :, :].rearrange("p h (k a) -> p (h k) a", a=16)
        tv = sb(B, "tv", [128, 8, 16])
        sel = sb(B, "sel", [128, 8, 16], U32)
        selu = sb(B, "selu", [128, 2, 128], U32)
        self_ = sb(B, "self", [128, 2, 128])
        ijg = sb(B, "ijg", [128, 3, 128])
        sm = sb(B, "sm", [128, 2, 8])
        ijgT = sb(B, "ijgT", [128, 3, 512])
        gs = Ring([Buf(sb(B, f"gs{i}", [128, 128, 32])) for i in range(2)])
        oneA = Ring([Buf(sb(B, f"oneA{i}", [128, 128])) for i in range(8)])
        oneB = Ring([Buf(sb(B, f"oneB{i}", [128, 128])) for i in range(8)])
        c_gs = [channel(f"c_gs{i}") for i in range(2)]

        t_rb = rms_scale([h[:, k, META:T] for k in range(KT)], t_hk, 512, D, sq)
        xf_ready = [scaled_split(h[:, k, META:T], g("g_ffn", k), 512, t_rb, tmp, XH[:, k, 0:512], XL[:, k, 0:512],
                                 pe.last()) for k in range(KT)]
        t_qp = []
        for m in range(8):
            (bank,), (t,) = gemm(XH, XL, FULL, xf_ready)
            te = act.op(lambda e, m=m, bank=bank: e.copy(qp[:, m, :], bank.t[:, :]), t)
            bank.free = [te]
            t_qp.append(te)

        def route(tt):
            q0 = tt * 128
            t_i = None
            for half in range(2):
                bp = [gemm_banks.next(), gemm_banks.next()]
                for p in range(2):
                    pe.wait(*bp[p].free, *t_qp, t_ky)
                    for i in range(4):
                        hd = half * 4 + i
                        t = pe.op(lambda e, p=p, i=i, hd=hd, bp=bp: e.matmul(
                            bp[p].t[:, i * 128:i * 128 + 128], qp[64 * p:64 * p + 64, hd, q0:q0 + 128],
                            ky[64 * p:64 * p + 64, hd, :], start=True, stop=True, skip_group_check=True))
                units = [(p, i, 2 * (half * 4 + i) + p) for i in range(4) for p in range(2)]
                dve.wait(t)
                w = [dve.op(lambda e, p=p, i=i, u=u, bp=bp: e.max(sv[:, u, 0:8], bp[p].t[:, i * 128:i * 128 + 128]))
                     for p, i, u in units]
                for j, (p, i, u) in enumerate(units):
                    dve.op(lambda e, p=p, i=i, u=u, bp=bp: e.max_index(siu[:, u, 0:8], sv[:, u, 0:8],
                                                                       bp[p].t[:, i * 128:i * 128 + 128]), w[j])
                x = [dve.op(lambda e, p=p, i=i, u=u, j=j, bp=bp: e.match_replace(
                    left[:, j, :], sv[:, u, 0:8], bp[p].t[:, i * 128:i * 128 + 128], TAKEN), w[j])
                    for j, (p, i, u) in enumerate(units)]
                bp[0].free = bp[1].free = [x[-1]]
                w = [dve.op(lambda e, u=u, j=j: e.max(sv[:, u, 8:16], left[:, j, :]), x[j])
                     for j, (p, i, u) in enumerate(units)]
                for j, (p, i, u) in enumerate(units):
                    t_i = dve.op(lambda e, u=u, j=j: e.max_index(siu[:, u, 8:16], sv[:, u, 8:16], left[:, j, :]), w[j])
            t_f = dve.op(lambda e: e.tensor_copy(sif[:, :, :], siu[:, :, :]), t_i)
            s4 = sv[:, :, :].rearrange("p (h q) a -> p h q a", q=2)
            t_cd = dve.op(lambda e: e.tensor_tensor(
                cand[:, :, :].rearrange("p h (a b) -> p h a b", a=16),
                s4[:, :, 0, :].unsqueeze(3).to_broadcast([128, 8, 16, 16]),
                s4[:, :, 1, :].unsqueeze(2).to_broadcast([128, 8, 16, 16]), ALU.add), t_i)
            w = [dve.op(lambda e, i=i: e.max(tv[:, i, 0:8], cand[:, i, :]), t_cd) for i in range(8)]
            for i in range(8):
                dve.op(lambda e, i=i: e.max_index(sel[:, i, 0:8], tv[:, i, 0:8], cand[:, i, :]), w[i])
            x = [dve.op(lambda e, i=i: e.match_replace(left2[:, i, :], tv[:, i, 0:8], cand[:, i, :], TAKEN), w[i])
                 for i in range(8)]
            w = [dve.op(lambda e, i=i: e.max(tv[:, i, 8:16], left2[:, i, :]), x[i]) for i in range(8)]
            for i in range(8):
                t_s = dve.op(lambda e, i=i: e.max_index(sel[:, i, 8:16], tv[:, i, 8:16], left2[:, i, :]), w[i])
            sf = sel[:, :, :].rearrange("p h k -> p (h k)")
            dve.op(lambda e: e.tensor_scalar(selu[:, 0, :], sf, 4, None, ALU.logical_shift_right), t_s)
            t = dve.op(lambda e: e.tensor_scalar(selu[:, 1, :], sf, 15, None, ALU.bitwise_and))
            t = dve.op(lambda e: e.tensor_copy(self_[:, :, :], selu[:, :, :]), t)
            si4 = sif[:, :, :].rearrange("p (h q) a -> p h q a", q=2)
            for q in range(2):
                t = dve.op(lambda e, q=q: e.tensor_tensor(
                    hot, self_[:, q, :].unsqueeze(2).to_broadcast([128, 128, 16]),
                    iota[:, 0:16].unsqueeze(1).to_broadcast([128, 128, 16]), ALU.is_equal), t)
                hv = left2[:, :, :].rearrange("p h (k a) -> p h k a", a=16)
                t = dve.op(lambda e, q=q, hv=hv: e.tensor_tensor(
                    hv, hv, si4[:, :, q, :].unsqueeze(2).to_broadcast([128, 8, 16, 16]), ALU.mult), t, t_f)
                t = dve.op(lambda e, q=q: e.tensor_reduce(ijg[:, q, :], hot, AX.X, ALU.add), t, ijg_free[0])
            gv = ijg[:, 2, :].rearrange("p (h k) -> p h k", h=8)
            t2 = dve.op(lambda e: e.tensor_tensor(gv, tv[:, :, :], tv[:, :, 0:1].to_broadcast([128, 8, 16]),
                                                  ALU.subtract), t_s, ijg_free[0])
            t2 = act.op(lambda e: e.activation(gv, gv, ACT.Exp), t2)
            t2 = dve.op(lambda e: e.tensor_reduce(sm[:, 0, :], gv, AX.X, ALU.add), t2)
            t2 = dve.op(lambda e: e.reciprocal(sm[:, 1, :], sm[:, 0, :]), t2)
            t2 = dve.op(lambda e: e.tensor_tensor(gv, gv, sm[:, 1, :].unsqueeze(2).to_broadcast([128, 8, 16]),
                                                  ALU.mult), t2)
            bank = gemm_banks.next()
            pe.wait(t, t2, *bank.free)
            for i in range(3):
                tp = pe.op(lambda e, i=i, bank=bank: e.transpose(bank.t[:, i * 128:i * 128 + 128], ijg[:, i, :],
                                                                 ident))
            ijg_free[0] = tp
            t = dve.op(lambda e, bank=bank: e.tensor_copy(
                ijgT[:, :, q0:q0 + 128], bank.t[:, 0:384].rearrange("p (i t) -> p i t", i=3)), tp)
            bank.free = [t]
            return t

        ijg_free = [None]
        t_g = []

        def scatter(tt, t_r):
            for blk in range(4 * tt, 4 * tt + 4):
                gbuf = gs.next()
                tg = []
                for q in range(8):
                    bank = gemm_banks.next()
                    for i in range(4):
                        t = blk * 32 + q * 4 + i
                        a, b = oneA.next(), oneB.next()
                        ta = dve.op(lambda e, a=a, t=t: e.tensor_scalar(a.t[:, :], iota, ijgT[:, 0, t:t + 1],
                                                                        ijgT[:, 2, t:t + 1], ALU.is_equal, ALU.mult),
                                    t_r, *a.free)
                        tb = pool.op(lambda e, b=b, t=t: e.tensor_scalar(b.t[:, :], iota, ijgT[:, 1, t:t + 1], None,
                                                                         ALU.is_equal), t_r, *b.free)
                        pe.wait(*bank.free)
                        tm = pe.op(lambda e, a=a, b=b, i=i, bank=bank: e.matmul(
                            bank.t[:, i * 128:i * 128 + 128], b.t[:, :], a.t[:, :], start=True, stop=True,
                            skip_group_check=True), ta, tb)
                        a.free = b.free = [tm]
                    te = act.op(lambda e, q=q, bank=bank, gbuf=gbuf: e.copy(
                        gbuf.t[:, :, q * 4:q * 4 + 4].rearrange("p i t -> p t i"),
                        bank.t[:, :].rearrange("p (t i) -> p t i", t=4)), tm, *gbuf.free)
                    bank.free = [te]
                t = c_gs[blk % 2].start(sp, gdram[:, blk, :, :], gbuf.t[:, :, :], te)
                gbuf.free = [t]
                t_g.append(t)

        for tt in range(4):
            scatter(tt, route(tt))
        dump("ijgT", ijgT[:, :, :])
        fence(*t_g[-2:])
        B.close()

        C = ExitStack()
        WTH = [sb(C, f"WTH{i}", [128, 8, 512], F32R) for i in range(2)]
        WTL = [sb(C, f"WTL{i}", [128, 8, 512], F32R) for i in range(2)]
        gr = Ring([Buf(sb(C, f"gr{i}", [128, 16, 8 * 32])) for i in range(2)])
        c_gr = [channel(f"c_gr{i}") for i in range(2)]
        ge = Ring([Buf(sb(C, f"ge{i}", [128, 512])) for i in range(3)])
        wt_free = [None, None]
        wt_ready = [None, None]

        def load_group(gi):
            b = gr.next()
            t = c_gr[gi % 2].start(sp, b.t[:, :, :],
                                   gdram[:, :, gi * 8:gi * 8 + 8, :].rearrange("p b i t -> p b (i t)"), *b.free)
            return b, t

        nxt = load_group(0)
        for gi in range(N_GROUPS + 1):
            if gi < N_GROUPS:
                gbuf, t_gr = nxt
                if gi + 1 < N_GROUPS:
                    nxt = load_group(gi + 1)
                s = gi % 2
                ready = []
                for i in range(8):
                    (bank,), (t,) = gemm(XH, XL, FULL, xf_ready)
                    b = ge.next()
                    t1 = act.op(lambda e, b=b, bank=bank: e.activation(b.t[:, :], bank.t[:, :], ACT.Gelu), t, *b.free)
                    bank.free = [t1]
                    t2 = dve.op(lambda e, b=b, i=i, gbuf=gbuf: e.tensor_tensor(
                        b.t[:, :].rearrange("p (b t) -> p b t", t=32), b.t[:, :].rearrange("p (b t) -> p b t", t=32),
                        gbuf.t[:, :, i * 32:i * 32 + 32], ALU.mult), t1, t_gr)
                    t3 = act.op(lambda e, b=b, i=i, s=s: e.copy(WTH[s][:, i, :], b.t[:, :]), t2, wt_free[s])
                    t4 = dve.op(lambda e, b=b, i=i, s=s: e.tensor_tensor(WTL[s][:, i, :], b.t[:, :],
                                                                         WTH[s][:, i, :].bitcast(F32), ALU.subtract),
                                t3, wt_free[s])
                    b.free = [t3, t4]
                    ready.append((t3, t4))
                gbuf.free = [t2]
                wt_ready[s] = ready
            if gi > 0:
                s = (gi - 1) % 2
                for m in range(8):
                    (bank,), (t,) = gemm(WTH[s], WTL[s], FULL, wt_ready[s])
                    tt = dve.op(lambda e, m=m, bank=bank: e.tensor_tensor(h[:, m, META:T], bank.t[:, :],
                                                                          h[:, m, META:T], ALU.add), t, t_hk[m])
                    bank.free = [tt]
                    t_hk[m] = tt
                wt_free[s] = t
        dump("h2", h[:, :, META:])
        fence()
        C.close()

        E = ExitStack()
        tmp = Ring([Buf(sb(E, f"etmp{i}", [128, 512])) for i in range(3)])
        sq = Ring([Buf(sb(E, f"esq{i}", [128, 512])) for i in range(2)])
        mixed = sb(E, "mixed", [128, 8, 512])
        ckvT = sb(E, "ckvT", [128, 512])
        ckv = sb(E, "ckv", [128, 4, 128])
        dt_ = [sb(E, f"dt{i}", [128, 128 * (i + 1)]) for i in range(1, 4)]
        uv = sb(E, "uv", [128, 16, 64])
        c_e = [channel(f"c_e{i}") for i in range(3)]
        t_uv = c_e[0].start(sp, uv[:, :, :], w_uv)
        hx = [h[:, k, META:T] for k in range(KT)]
        t_rb = rms_scale(hx, t_hk, 512, D, sq)
        for k in range(KT):
            t_hk[k] = dve.op(lambda e, k=k: e.scalar_tensor_tensor(hx[k], hx[k], g("g_fin", k), rb[:, 0:512],
                                                                   ALU.mult, ALU.mult), t_rb)
        rb_free[0] = t_hk[-1]
        t_rb = rms_scale(hx, t_hk, 512, D, sq)
        x2_ready = [scaled_split(hx[k], g("g2", k), 512, t_rb, tmp, XH[:, k, 0:512], XL[:, k, 0:512]) for k in range(KT)]
        dump("x2", h[:, :, META:])

        R = ExitStack()
        hgh = sb(R, "hgh", [128, 8, 512], F32R)
        hgl = sb(R, "hgl", [128, 8, 512], F32R)
        qi = sb(R, "qi", [128, 4, 512])
        kx = sb(R, "kx", [128, 512])
        wx = sb(R, "wx", [128, 4, 8])
        rg = sb(R, "rg", [128, 2, 8, 128])
        t_rg = c_e[1].start(sp, rg[:, :, :, :], w_rg)
        sidx = [sb(R, f"sidx{i}", [128, 128 * (i + 1)]) for i in range(1, 4)]
        top8 = Ring([Buf(sb(R, f"top8_{i}", [128, 8])) for i in range(6)])
        rt = [Buf(sb(R, f"rt{i}", [128, 515])) for i in range(4)]

        t_qi = []
        for i in range(4):
            (bank,), (t,) = gemm(XH, XL, FULL, x2_ready)
            te = act.op(lambda e, i=i, bank=bank: e.mul(qi[:, i, :], bank.t[:, :], 0.125), t)
            bank.free = [te]
            t_qi.append(te)
        (bank,), (t,) = gemm(XH, XL, FULL, x2_ready)
        te = act.op(lambda e, bank=bank: e.copy(kx[0:96, :], bank.t[0:96, :]), t)
        bank.free = [te]
        u = tmp.next()
        tw = dve.op(lambda e, u=u: e.tensor_scalar(u.t[64:96, :], kx[64:96, :], 8.0 ** -0.5, None, ALU.mult), te,
                     *u.free)
        bank = gemm_banks.next()
        pe.wait(tw, *bank.free)
        for j in range(4):
            t = pe.op(lambda e, j=j, u=u, bank=bank: e.matmul(
                bank.t[:, j * 8:j * 8 + 8], u.t[64:96, j * 128:j * 128 + 128], ident[64:96, 64:72],
                start=True, stop=True, skip_group_check=True))
        t_wx = act.op(lambda e, bank=bank: e.copy(wx[:, :, :], bank.t[:, 0:32].rearrange("p (j w) -> p j w", w=8)), t)
        bank.free = [t_wx]
        u.free = [t]
        bank = gemm_banks.next()
        t = mm_group([(bank.t[:, :], inv64[0:64, :], kx[0:64, :])], te, *bank.free)
        t = dve.op(lambda e, bank=bank: e.tensor_tensor(kx[0:64, :], kx[0:64, :], bank.t[0:64, :], ALU.subtract), t)
        bank.free = [t]
        t_rb = rms_scale([kx[0:64, :]], [t], 512, 64, sq, rows=64)
        t = dve.op(lambda e: e.scalar_tensor_tensor(kx[0:64, :], kx[0:64, :], gn[0:64, GCOL["g_idx"]:GCOL["g_idx"] + 1],
                                                    rb[0:64, 0:512], ALU.mult, ALU.mult), t_rb)
        rb_free[0] = t
        t = dve.op(lambda e: e.tensor_scalar(kx[0:64, :], kx[0:64, :], gn[0:64, GCOL["b_idx"]:GCOL["b_idx"] + 1], None,
                                             ALU.add), t)
        t_kx = act.op(lambda e: e.copy(kx[64:128, :], kx[0:64, :]), t, tw)
        dump("kx", kx[:, :])

        t_si = [None] * 3
        for j in range(8):
            p0 = 64 * (j % 2)
            for qt in range(1, 4):
                n = 128 * (qt + 1)
                bank = gemm_banks.next()
                t = mm_group([(bank.t[:, 0:n], qi[p0:p0 + 64, j // 2, qt * 128:qt * 128 + 128], kx[p0:p0 + 64, 0:n])],
                             t_kx, *t_qi, *bank.free)
                u = tmp.next()
                tr = act.op(lambda e, u=u, bank=bank, n=n: e.activation(u.t[:, 0:n], bank.t[:, 0:n], ACT.Relu), t,
                            *u.free)
                bank.free = [tr]
                so = sidx[qt - 1][:, :]
                if j == 0:
                    ta = dve.op(lambda e, u=u, so=so, n=n, qt=qt: e.tensor_scalar(so, u.t[:, 0:n], wx[:, qt, 0:1],
                                                                                  None, ALU.mult), tr, t_wx)
                else:
                    ta = dve.op(lambda e, u=u, so=so, n=n, qt=qt, j=j: e.scalar_tensor_tensor(
                        so, u.t[:, 0:n], wx[:, qt, j:j + 1], so, ALU.mult, ALU.add), tr, t_si[qt - 1])
                u.free = [ta]
                t_si[qt - 1] = ta
        for qt in range(1, 4):
            so = sidx[qt - 1]
            t_si[qt - 1] = dve.op(lambda e, so=so, qt=qt: e.tensor_tensor(
                so[:, qt * 128:qt * 128 + 128], so[:, qt * 128:qt * 128 + 128], cmask, ALU.add), t_si[qt - 1])
            dump(f"sidx{qt}", so[:, :])

        rounds = [r for r in range(16)]

        def topk_round():
            if not rounds:
                return
            rounds.pop(0)
            bs = [top8.next() for _ in range(3)]
            ts = [dve.op(lambda e, b=b, i=i: e.max(b.t[:, :], sidx[i][:, :]), t_si[i], *b.free)
                  for i, b in enumerate(bs)]
            for i, b in enumerate(bs):
                t_si[i] = dve.op(lambda e, b=b, i=i: e.match_replace(sidx[i][:, :], b.t[:, :], sidx[i][:, :], TAKEN),
                                 ts[i])
                b.free = [t_si[i]]

        (bank,), (t,) = gemm(XH, XL, FULL, x2_ready)
        te = act.op(lambda e, bank=bank: e.copy(ckvT[:, :], bank.t[:, :]), t)
        bank.free = [te]
        t_rb = rms_scale([ckvT[:, :]], [te], 512, 128, sq)
        t_ct = dve.op(lambda e: e.scalar_tensor_tensor(ckvT[:, :], ckvT[:, :], g("g_kv2"), rb[:, 0:512],
                                                       ALU.mult, ALU.mult), t_rb)
        rb_free[0] = t_ct
        bank = gemm_banks.next()
        pe.wait(t_ct, *bank.free)
        for j in range(4):
            t = pe.op(lambda e, j=j, bank=bank: e.transpose(bank.t[:, j * 128:j * 128 + 128],
                                                            ckvT[:, j * 128:j * 128 + 128], ident))
        t_ck = act.op(lambda e, bank=bank: e.copy(ckv[:, :, :], bank.t[:, :].rearrange("p (j c) -> p j c", c=128)), t)
        bank.free = [t_ck]

        sps = sb(R, "sps", [128, 8, 8])
        lam = gn[:, GCOL["lam"]:GCOL["lam"] + 8]
        dve.op(lambda e: e.tensor_scalar(sps[:, 0, :], lam, -1.0, 0.0, ALU.mult, ALU.max))
        t = act.op(lambda e: e.activation(sps[:, 1, :], lam, ACT.Abs))
        t = act.op(lambda e: e.activation(sps[:, 1, :], sps[:, 1, :], ACT.Exp, scale=-1.0), t)
        t = dve.op(lambda e: e.tensor_scalar(sps[:, 2, :], sps[:, 1, :], 1.0, None, ALU.add), t)
        tl = act.op(lambda e: e.activation(sps[:, 3, :], sps[:, 2, :], ACT.Ln), t)
        t = dve.op(lambda e: e.tensor_scalar(sps[:, 4, :], sps[:, 2, :], -1.0, None, ALU.add), t)
        t = dve.op(lambda e: e.tensor_scalar(sps[:, 5, :], sps[:, 4, :], 0.0, None, ALU.is_equal), t)
        t = dve.op(lambda e: e.tensor_tensor(sps[:, 4, :], sps[:, 4, :], sps[:, 5, :], ALU.add), t)
        t = dve.op(lambda e: e.reciprocal(sps[:, 4, :], sps[:, 4, :]), t)
        t = dve.op(lambda e: e.tensor_tensor(sps[:, 3, :], sps[:, 3, :], sps[:, 5, :], ALU.add), t, tl)
        t = dve.op(lambda e: e.tensor_tensor(sps[:, 4, :], sps[:, 4, :], sps[:, 3, :], ALU.mult), t)
        t = dve.op(lambda e: e.tensor_tensor(sps[:, 4, :], sps[:, 4, :], sps[:, 1, :], ALU.mult), t)
        t = dve.op(lambda e: e.tensor_tensor(sps[:, 4, :], sps[:, 4, :], sps[:, 0, :], ALU.add), t)
        t = dve.op(lambda e: e.tensor_scalar(sps[:, 6, :], sps[:, 4, :], -8.0, None, ALU.mult), t)
        t_sp = dve.op(lambda e: e.tensor_scalar(sps[:, 7, :], sps[:, 4, :], 8.0, None, ALU.mult), t)
        for r_ in rt:
            r_.free = []

        xr, gr_, b2_, b3_ = rt
        t_pad = pool.op(lambda e: e.memset(xr.t[:, 0:3], 0.0))
        hg_ready = []
        last = [None] * 8
        pe.wait(t_rg)
        fx = [None] * 6
        for c in range(8):
            (bank,), (t,) = gemm(XH, XL, FULL, x2_ready)
            tx = act.op(lambda e, bank=bank: e.copy(xr.t[:, 3:515], bank.t[:, :]), t, fx[0])
            bank.free = [tx]
            w = lambda k, c=c: g("conv_w2", c * 4 + k)
            xc = tmp.next()
            t = dve.op(lambda e, c=c, xc=xc, w=w: e.tensor_scalar(xc.t[:, :], xr.t[:, 0:512], w(0), g("conv_b2", c),
                                                                  ALU.mult, ALU.add), tx, t_pad, *xc.free)
            for k in range(1, 4):
                t = dve.op(lambda e, k=k, xc=xc, w=w: e.scalar_tensor_tensor(
                    xc.t[:, :], xr.t[:, k:k + 512], w(k), xc.t[:, :], ALU.mult, ALU.add), t)
            fx[0] = t
            ba, bx = gemm_banks.next(), gemm_banks.next()
            ta = mm_group([(ba.t[:, :], rg[:, 0, c, :], xc.t[:, :])], t, *ba.free)
            tb = mm_group([(bx.t[:, :], rg[:, 1, c, :], xc.t[:, :])], t, *bx.free)
            tr = act.op(lambda e, c=c, ba=ba: e.activation(b2_.t[:, 0:512], ba.t[:, :], ACT.Sigmoid, bias=g("b_a", c)),
                        ta, fx[1])
            ti = act.op(lambda e, c=c, bx=bx: e.activation(b3_.t[:, 0:512], bx.t[:, :], ACT.Sigmoid, bias=g("b_x", c)),
                        tb, fx[2])
            ba.free, bx.free = [tr], [ti]
            tix = dve.op(lambda e, xc=xc: e.tensor_tensor(xc.t[:, :], b3_.t[:, 0:512], xc.t[:, :], ALU.mult), ti)
            tt1 = act.op(lambda e, c=c: e.activation(b3_.t[:, 0:512], b2_.t[:, 0:512], ACT.Tanh,
                                                     scale=sps[:, 7, c:c + 1]), tr, tix, t_sp)
            tt2 = act.op(lambda e, c=c: e.activation(b2_.t[:, 0:512], b2_.t[:, 0:512], ACT.Exp,
                                                     scale=sps[:, 6, c:c + 1]), tt1)
            y = tmp.next()
            t = dve.op(lambda e, y=y: e.tensor_scalar(y.t[:, :], b3_.t[:, 0:512], 1.0, None, ALU.add), tt1, *y.free)
            t = dve.op(lambda e, y=y: e.reciprocal(y.t[:, :], y.t[:, :]), t)
            t = dve.op(lambda e, y=y: e.scalar_tensor_tensor(y.t[:, :], b3_.t[:, 0:512], 2.0, y.t[:, :], ALU.mult,
                                                             ALU.mult), t)
            t = act.op(lambda e, y=y: e.sqrt(y.t[:, :], y.t[:, :]), t)
            t = dve.op(lambda e, y=y, xc=xc: e.tensor_tensor(y.t[:, :], y.t[:, :], xc.t[:, :], ALU.mult), t, tix)
            xc.free = [t, tb]
            t = dve.op(lambda e, y=y: e.tensor_tensor_scan(b3_.t[:, 0:512], b2_.t[:, 0:512], y.t[:, :], 0.0,
                                                           ALU.mult, ALU.add), t, tt2)
            y.free = [t]
            fx[1] = t
            t_scan = t
            (bank,), (t,) = gemm(XH, XL, FULL, x2_ready)
            ts = act.op(lambda e, bank=bank: e.activation(gr_.t[:, 0:512], bank.t[:, :], ACT.Silu), t, fx[3])
            bank.free = [ts]
            t = dve.op(lambda e: e.tensor_tensor(gr_.t[:, 0:512], gr_.t[:, 0:512], b3_.t[:, 0:512], ALU.mult), ts,
                       t_scan)
            fx[2] = t
            sp_ = split(gr_.t[:, 0:512], t, hgh[:, c, :], hgl[:, c, :])
            hg_ready.append(sp_)
            fx[3] = sp_[1]
            topk_round()
        while rounds:
            topk_round()
        t_dt = [None]
        for qt in range(1, 4):
            n = 128 * (qt + 1)
            so, do = sidx[qt - 1], dt_[qt - 1]
            t = dve.op(lambda e, so=so, n=n: e.tensor_scalar(so[:, :], so[:, :], TAKEN, -1.0, ALU.is_equal, ALU.add),
                       t_si[qt - 1])
            t_dt.append(dve.op(lambda e, so=so, do=do, qt=qt: e.scalar_tensor_tensor(
                do[:, :], so[:, :], BIG, dist[:, 384 - 128 * qt:512], ALU.mult, ALU.add), t))

        for m in range(8):
            (bm,), (tm,) = gemm(XH, XL, FULL, x2_ready)
            (by,), (ty,) = gemm(hgh, hgl, FULL, hg_ready)
            u = tmp.next()
            ts = act.op(lambda e, m=m, u=u, bm=bm: e.activation(u.t[:, :], bm.t[:, :], ACT.Sigmoid,
                                                                bias=g("b_merge", 8 + m)), tm, *u.free)
            bm.free = [ts]
            t_mix = dve.op(lambda e, m=m, u=u, by=by: e.tensor_tensor(mixed[:, m, :], by.t[:, :], u.t[:, :],
                                                                      ALU.mult), ts, ty)
            by.free = [t_mix]
            u.free = [t_mix]
        dump("mixed", mixed[:, :, :])
        fence()
        R.close()

        G = ExitStack()
        qT = sb(G, "qT", [128, 8, 512])
        qlr = Ring([Buf(sb(G, f"ql{i}", [128, 512])) for i in range(2)])
        ga = sb(G, "ga", [128, 8, 512])
        ma = sb(G, "ma", [128, 8, 512])
        uk = sb(G, "uk", [128, 8, 128])
        t_uk = c_e[2].start(sp, uk[:, :, :], w_uk)
        for m in range(8):
            (bank,), (t,) = gemm(XH, XL, FULL, x2_ready)
            t_q = act.op(lambda e, m=m, bank=bank: e.copy(qT[:, m, :], bank.t[:, :]), t)
            bank.free = [t_q]
        for m in range(8):
            (bank,), (t,) = gemm(XH, XL, FULL, x2_ready)
            te = act.op(lambda e, m=m, bank=bank: e.activation(ga[:, m, :], bank.t[:, :], ACT.Silu), t)
            bank.free = [te]
        t_ga = te
        for m in range(8):
            (bank,), (t,) = gemm(XH, XL, FULL, x2_ready)
            te = act.op(lambda e, m=m, bank=bank: e.activation(ma[:, m, :], bank.t[:, :], ACT.Sigmoid,
                                                               bias=g("b_merge", m)), t)
            bank.free = [te]
        t_ma = te
        x_used = pe.last()

        fence()
        Pb = Ring(sq.bufs + [Buf(sb(G, "eP", [128, 512]))])
        PTb = Ring([Buf(sb(G, f"ePT{i}", [128, 1280])) for i in range(2)])
        mx = Ring([Buf(sb(G, f"emx{i}", [128, 4])) for i in range(6)])
        PTO = [0, 512, 896, 1152]
        og_ready = [None] * 8
        att_banks = Ring(banks[0:3])
        for hd in range(16):
            slope = float(np.exp2(np.float32(-8.0 * (hd + 1) / 16)))
            pt = PTb.next()
            ql = qlr.next()
            b0 = 64 * (hd % 2)
            bank = att_banks.next()
            t = mm_group([(bank.t[:, :], uk[b0:b0 + 64, hd // 2, :], qT[b0:b0 + 64, hd // 2, :])], t_q, t_uk,
                         *bank.free)
            t_ql = act.op(lambda e, ql=ql, bank=bank: e.mul(ql.t[:, :], bank.t[:, :], 0.125), t, *ql.free)
            bank.free = [t_ql]
            for qt in range(4):
                n = 128 * (qt + 1)
                bank = att_banks.next()
                tS = mm_group([(bank.t[:, 0:n], ql.t[:, qt * 128:qt * 128 + 128], ckvT[:, 0:n])], t_ql, t_ct,
                              *bank.free)
                P = Pb.next()
                m = mx.next()
                dd = dist[:, 384:512] if qt == 0 else dt_[qt - 1][:, :]
                t5 = dve.op(lambda e, P=P, dd=dd, bank=bank, n=n, slope=slope: e.scalar_tensor_tensor(
                    P.t[:, 0:n], dd, slope, bank.t[:, 0:n], ALU.mult, ALU.add), tS, t_dt[qt], *P.free)
                bank.free = [t5]
                t6 = dve.op(lambda e, m=m, P=P, n=n: e.tensor_reduce(m.t[:, 0:1], P.t[:, 0:n], AX.X, ALU.max,
                                                                     negate=True), t5, *m.free)
                t7 = act.op(lambda e, m=m, n=n, P=P: e.activation(P.t[:, 0:n], P.t[:, 0:n], ACT.Exp, bias=m.t[:, 0:1],
                                                                  accum_out=m.t[:, 1:2]), t6)
                t8 = dve.op(lambda e, m=m: e.reciprocal(m.t[:, 2:3], m.t[:, 1:2]), t7)
                t9 = dve.op(lambda e, m=m, P=P, n=n: e.tensor_scalar(P.t[:, 0:n], P.t[:, 0:n], m.t[:, 2:3], None,
                                                                     ALU.mult), t8)
                m.free = [t9]
                wb = wide_banks.next()
                pe.wait(t9, *wb.free)
                for i in range(qt + 1):
                    f = lambda e, wb=wb, P=P, i=i: e.transpose(wb.t[:, i * 128:i * 128 + 128],
                                                               P.t[:, i * 128:i * 128 + 128], ident)
                    if i < qt:
                        pe.silent(f)
                tT = pe.op(f)
                P.free = [tT]
                for i in range(qt + 1):
                    a = PTO[i] + (qt - i) * 128
                    tb_ = act.op(lambda e, wb=wb, pt=pt, a=a, i=i: e.copy(
                        pt.t[:, a:a + 128], wb.t[:, i * 128:i * 128 + 128]), tT, *pt.free)
                wb.free = [tb_]
            bank = att_banks.next()
            pe.wait(tb_, t_ck, *bank.free)
            for i in range(4):
                f = lambda e, i=i, pt=pt, bank=bank: e.matmul(bank.t[:, i * 128:512], ckv[:, i, :],
                                                              pt.t[:, PTO[i]:PTO[i] + 512 - 128 * i],
                                                              start=(i == 0), stop=(i == 3), skip_group_check=True)
                if i < 3:
                    pe.silent(f)
            tO = pe.op(f)
            pt.free = [tO]
            ql.free = [tO]
            ol = tmp.next()
            te = act.op(lambda e, ol=ol, bank=bank: e.copy(ol.t[:, :], bank.t[:, :]), tO, *ol.free)
            bank.free = [te]
            if hd % 2 == 0:
                pair = banks[3]
            pe.wait(te, t_uv, *pair.free)
            tO = pe.op(lambda e, pair=pair, b0=b0, hd=hd, ol=ol: e.matmul(pair.t[b0:b0 + 64, :], uv[:, hd, :],
                                                                          ol.t[:, :], start=True, stop=True,
                                                                          skip_group_check=True))
            ol.free = [tO]
            if hd % 2 == 1:
                c = hd // 2
                u = tmp.next()
                t = dve.op(lambda e, c=c, u=u, pair=pair: e.tensor_tensor(u.t[:, :], pair.t[:, :], ga[:, c, :],
                                                                          ALU.mult), tO, t_ga, *u.free)
                pair.free = [t]
                r_ = split(u.t[:, :], t, XH[:, c, 0:512], XL[:, c, 0:512], x_used)
                u.free = list(r_)
                og_ready[c] = r_
        t_mx = []
        for m in range(8):
            (bank,), (t,) = gemm(XH, XL, FULL, og_ready)
            u = tmp.next()
            t1 = dve.op(lambda e, m=m, u=u, bank=bank: e.tensor_tensor(u.t[:, :], bank.t[:, :], ma[:, m, :], ALU.mult),
                        t, t_ma, *u.free)
            bank.free = [t1]
            t2 = dve.op(lambda e, m=m, u=u: e.tensor_tensor(mixed[:, m, :], u.t[:, :], mixed[:, m, :], ALU.add),
                        t1, t_mix)
            u.free = [t2]
            t_mx.append(t2)
        last_y = pe.last()
        mix_ready = [split(mixed[:, m, :], t_mx[m], XH[:, m, 0:512], XL[:, m, 0:512], last_y) for m in range(8)]
        for m in range(8):
            (bank,), (t,) = gemm(XH, XL, FULL, mix_ready)
            tt = dve.op(lambda e, m=m, bank=bank: e.tensor_tensor(hx[m], bank.t[:, :], hx[m], ALU.add), t)
            bank.free = [tt]
            t_hk[m] = tt
        t_rb = rms_scale(hx, t_hk, 512, D, sq)
        c_out = channel("c_out")
        for k in range(KT):
            t = dve.op(lambda e, k=k: e.scalar_tensor_tensor(hx[k], hx[k], g("g_fin2", k), rb[:, 0:512],
                                                             ALU.mult, ALU.mult), t_rb)
            t_out = c_out.start(sp, out[:, k, :], hx[k], t)
        sp.wait(t_out)
        G.close()
        E.close()

        block = ctx.enter_context(nc.Block())

        def run(engine):
            def body(e):
                for f in engine.queue:
                    f(e)
            return body

        block.tensor(run(pe))
        block.vector(run(dve))
        block.scalar(run(act))
        block.gpsimd(run(pool))
        block.sync(run(sp))


def _tiles(w):
    k, m = w.shape
    return w.reshape(k // 128, 128, m // 128, 128).transpose(2, 1, 0, 3).reshape(m // 128, 128, k)


def _cols(v):
    return v.reshape(-1, 128).T


def _constants():
    p = np.arange(128)[:, None]
    q = np.arange(128)[None, :]
    x = np.arange(512)[None, :]
    c = np.zeros((128, 1024), np.float32)
    c[:, 0:128] = p == q
    c[:, 128:256] = np.where(q <= p, 0.0, -BIG)
    c[:, 256:384] = q
    c[:, 384:896] = np.where(x - 384 - p <= 0, x - 384 - p, -BIG)
    c[:, 896:1024] = 1.0
    t = np.zeros((128, T), np.float32)
    freqs = np.float32(10000.0) ** (-np.arange(16, dtype=np.float32) / np.float32(16))
    ang = np.arange(T, dtype=np.float32)[:, None] * freqs[None, :].astype(np.float32)
    cos, sin = np.cos(ang).T, np.sin(ang).T
    t[64:80] = t[80:96] = cos
    t[96:112] = -sin
    t[112:128] = sin
    return c, t


def layouts(a):
    f = np.float32
    zeros = lambda *s: np.zeros(s, f)
    hT = np.concatenate([a["meta"], a["x"][0]], 0).T.reshape(8, 128, T).transpose(1, 0, 2)
    w_in = a["w_in"][0]
    r = w_in[:, 1408:1440]
    rope = np.concatenate([zeros(D, 64), r, r[:, 16:], r[:, :16]], 1)
    first = [w_in[:, 1024:1280], w_in[:, 1280:1408], rope]
    for c in range(4):
        first += [w_in[:, c * 128:c * 128 + 128], w_in[:, 512 + c * 128:640 + c * 128]]
    parts = [_tiles(np.concatenate(first, 1)), _tiles(a["w_out"][0]), _tiles(a["peer_wq"][0])]
    U = a["peer_u"][0].reshape(128, 128, 8, 128).transpose(0, 3, 2, 1).reshape(16, 8, 128, 1024)
    V = a["peer_v"][0].reshape(16, 8, 128, 8, 128).transpose(0, 3, 2, 1, 4).reshape(16, 8, 128, 1024)
    for gi in range(N_GROUPS + 1):
        if gi < N_GROUPS:
            parts.append(U[gi])
        if gi > 0:
            parts.append(V[gi - 1])
    w2 = a["w_in_2"][0]
    o = np.cumsum([0, 1024, 128, 512, 64, 8, 1024, 1024, 1024, 2048])
    q, ckv, qi, ki, wi, ga, xr, gr, mg = [w2[:, o[i]:o[i + 1]] for i in range(9)]
    parts.append(_tiles(np.concatenate([qi, ki, wi, zeros(D, 56), ckv], 1)))
    xr, gr, mg, rp = _tiles(xr), _tiles(gr), _tiles(mg), _tiles(a["w_rnn_proj_2"][0])
    parts.append(np.stack([xr, gr], 1).reshape(16, 128, 1024))
    parts.append(np.stack([mg[8:], rp], 1).reshape(16, 128, 1024))
    parts += [_tiles(q), _tiles(ga), mg[:8], _tiles(a["w_attn_proj_2"][0]), _tiles(a["w_out_2"][0])]
    wstream = np.concatenate(parts, 0)

    uq = a["w_uq"][0].reshape(2, 128, 8, 96)
    uq = np.concatenate([uq, uq[..., 80:96], uq[..., 64:80]], -1).transpose(1, 2, 0, 3).reshape(128, 2048)
    keys = a["peer_keys"][0].transpose(1, 3, 0, 2).reshape(128, 8, 128)
    uk = a["w_uk_2"][0].reshape(8, 2, 128, 64).transpose(1, 3, 0, 2).reshape(128, 8, 128)
    uv = a["w_uv_2"][0].transpose(1, 0, 2)
    rg = zeros(128, 2, 8, 128)
    for i, n in enumerate(("w_rg_a_2", "w_rg_x_2")):
        w = a[n][0].reshape(8, 2, 64, 64).transpose(1, 2, 0, 3)
        rg[0:64, i, :, 0:64] = w[0]
        rg[64:128, i, :, 64:128] = w[1]
    pad64 = lambda v: np.concatenate([v, zeros(64)])
    gv = {
        "g_mix": a["g_mix_norm"][0], "g_q": a["g_q"][0], "g_kv": a["g_kv"][0], "conv_b": a["conv_b"][0],
        "g_ln": a["g_conv_ln"][0], "b_ln": a["b_conv_ln"][0], "g_oa": a["g_out_attn"][0],
        "g_oc": a["g_out_conv"][0], "g_ffn": a["g_ffn_norm"][0], "g_fin": a["g_final"],
        "g2": a["norm_gain_2"][0], "b_merge": a["b_merge_2"][0], "g_kv2": a["kv_norm_gain_2"][0],
        "g_idx": pad64(a["idx_ln_gain_2"][0]), "b_idx": pad64(a["idx_ln_bias_2"][0]),
        "conv_b2": a["conv_b_2"][0], "b_a": a["b_rg_a_2"][0], "b_x": a["b_rg_x_2"][0],
        "lam": a["lru_lambda_2"][0], "g_fin2": a["final_norm_gain_2"],
    }
    cols = []
    for name, n in GAINS:
        if name == "conv_w":
            cols.append(a["conv_w"][0].reshape(31, 4, 128).transpose(2, 1, 0).reshape(128, 124))
        elif name == "conv_w2":
            cols.append(a["conv_w_2"][0].reshape(4, 8, 128).transpose(2, 1, 0).reshape(128, 32))
        else:
            cols.append(_cols(gv[name]))
    c, t = _constants()
    return {
        "hT": hT, "wstream": wstream, "gains": np.concatenate(cols, 1), "consts": c, "trig": t, "w_uq": uq,
        "w_ukv": a["w_ukv"][0], "keys": keys, "w_uk": uk, "w_uv": uv, "w_rg": rg,
    }


def kernel(**inputs):
    import concourse.bacc as _bacc
    from concourse.bass_utils import run_bass_kernel_spmd as _run

    a = {k: np.asarray(v) for k, v in inputs.items()}
    arrays = {k: np.ascontiguousarray(v) for k, v in layouts(a).items()}
    nc = _bacc.Bacc("TRN2", target_bir_lowering=False, num_devices=1)
    args = {k: nc.dram_tensor(f"in_{k}", v.shape, F32, kind="ExternalInput").ap() for k, v in arrays.items()}
    out = nc.dram_tensor("out_0", (128, 8, 512), F32, kind="ExternalOutput").ap()
    build_program(nc, out=out, **args)
    r = _run(nc, [{f"in_{k}": v for k, v in arrays.items()}], core_ids=[0])
    y = np.asarray(r.results[0]["out_0"])
    return np.ascontiguousarray(y.transpose(1, 0, 2).reshape(1024, 512).T)[None]
```

```python
from contextlib import ExitStack

import numpy as np

import concourse.bass as bass
from concourse import mybir

F32 = mybir.dt.float32
F32R = mybir.dt.float32r
BF16 = mybir.dt.bfloat16
U32 = mybir.dt.uint32
ALU = mybir.AluOpType
ACT = mybir.ActivationFunctionType
AX = mybir.AxisListType

D = 1024
META = 16
S = 512
T = META + S
KT = D // 128
EPS = 1e-6
BIG = 1e30
TAKEN = -3e38

GAINS = [
    ("g_mix", 8), ("g_q", 2), ("g_kv", 1), ("conv_w", 4 * 31), ("conv_b", 4), ("g_ln", 4), ("b_ln", 4),
    ("g_oa", 4), ("g_oc", 4), ("g_ffn", 8), ("g_fin", 8), ("g2", 8), ("b_merge", 16), ("g_kv2", 1),
    ("g_idx", 1), ("b_idx", 1), ("conv_w2", 8 * 4), ("conv_b2", 8), ("b_a", 8), ("b_x", 8), ("lam", 8),
    ("g_fin2", 8),
]
GCOL = {}
NG = 0
for _name, _n in GAINS:
    GCOL[_name] = NG
    NG += _n

N_GROUPS = 16
SPILLED = 9
ORDER = [SPILLED] + list(range(SPILLED)) + list(range(SPILLED + 1, N_GROUPS))
N_TILES = 12 + 8 + 8 + 128 + 128 + 54 + 8 * 3


def expert_steps():
    for i in range(8):
        yield "U", 0, i
    for n in range(N_GROUPS):
        for m in range(8):
            if n + 1 < N_GROUPS:
                if m == 0:
                    yield "U", n + 1, 0
                if m < 7:
                    yield "U", n + 1, m + 1
            yield "V", n, m


class Engine:

    def __init__(self, sem):
        self.sem = sem
        self.count = 0
        self.queue = []
        self.reached = {}

    def wait(self, *tokens):
        for token in tokens:
            if token is None:
                continue
            sem, value = token
            if self.reached.get(sem, 0) < value:
                self.reached[sem] = value
                self.queue.append(lambda e, s=sem, v=value: e.wait_ge(s, v))

    def op(self, fn, *tokens):
        self.wait(*tokens)
        self.count += 1
        self.queue.append(lambda e: fn(e).then_inc(self.sem, 1))
        return (self.sem, self.count)

    def silent(self, fn, *tokens):
        self.wait(*tokens)
        self.queue.append(fn)

    def last(self):
        return (self.sem, self.count) if self.count else None


class Channel:

    def __init__(self, sem):
        self.sem = sem
        self.count = 0

    def start(self, engine, out, in_, *tokens):
        engine.wait(*tokens)
        self.count += 16
        engine.queue.append(lambda e: e.dma_start(out, in_).then_inc(self.sem, 16))
        return (self.sem, self.count)

    def last(self):
        return (self.sem, self.count)


class Buf:

    def __init__(self, t):
        self.t = t
        self.free = []


class Ring:
    def __init__(self, bufs):
        self.bufs = bufs
        self.at = 0

    def next(self):
        b = self.bufs[self.at % len(self.bufs)]
        self.at += 1
        return b


def build_program(nc, hT, wstream, gains, consts, trig, w_uq, w_ukv, keys, w_uk, w_uv, w_rg, out, dbg=None):
    gdram = nc.dram_tensor("g_scratch", (128, 16, 128, 32), F32, kind="Internal").ap()
    adram = nc.dram_tensor("a_scratch", (128, SPILLED * 8, 512), F32, kind="Internal").ap()
    ctx = ExitStack()
    with ctx:
        def sem(name):
            return ctx.enter_context(nc.semaphore(name))

        def sb(stack, name, shape, dt=F32):
            return stack.enter_context(nc.sbuf_tensor(name, shape, dt))

        pe = Engine(sem("s_pe"))
        dve = Engine(sem("s_dve"))
        act = Engine(sem("s_act"))
        pool = Engine(sem("s_pool"))
        sp = Engine(sem("s_sp"))
        engines = [pe, dve, act, pool]

        def channel(name):
            return Channel(sem(name))

        def fence(*more):
            tokens = [e.last() for e in engines] + list(more)
            for e in (dve, act, pool, sp):
                e.wait(*tokens)
            return tokens

        banks = [Buf(ctx.enter_context(nc.psum_tensor(f"bank{i}", [128, 512], F32))) for i in range(4)]
        wide = [Buf(ctx.enter_context(nc.psum_tensor(f"wide{i}", [128, 1024], F32))) for i in range(2)]
        gemm_banks = Ring(banks)
        wide_banks = Ring(wide)

        h = sb(ctx, "h", [128, KT, T])
        XH = sb(ctx, "XH", [128, KT, T], F32R)
        XL = sb(ctx, "XL", [128, KT, T], F32R)
        NRAW, NSPLIT = 4, 3
        wraw = [sb(ctx, f"wraw{i}", [128, 1024]) for i in range(NRAW)]
        wh = [sb(ctx, f"wh{i}", [128, 1024], F32R) for i in range(NSPLIT)]
        wl = [sb(ctx, f"wl{i}", [128, 1024], F32R) for i in range(NSPLIT)]
        gn = sb(ctx, "gn", [128, NG])
        cst = sb(ctx, "cst", [128, 1024])
        ident = cst[:, 0:128]
        cmask = cst[:, 128:256]
        iota = cst[:, 256:384]
        dist = cst[:, 384:896]
        ones = cst[:, 896:1024]
        identb = sb(ctx, "identb", [128, 128], BF16)
        cmaskb = sb(ctx, "cmaskb", [128, 128], BF16)
        st = sb(ctx, "st", [128, 4, 8])
        st_gg = sb(ctx, "st_gg", [128, 8])
        tmp = Ring([Buf(sb(ctx, f"tmp{i}", [128, T])) for i in range(3)])
        sq = Ring([Buf(sb(ctx, f"sq{i}", [128, T])) for i in range(2)])
        either = Ring(tmp.bufs + sq.bufs)
        diag = sb(ctx, "diag", [128, 5, 128])
        rb = sb(ctx, "rb", [128, T])
        inv512 = sb(ctx, "inv512", [128, 128])
        inv64 = sb(ctx, "inv64", [128, 128])
        st_free = [None]
        rb_free = [None]

        def g(name, i=0):
            c = GCOL[name] + i
            return gn[:, c:c + 1]

        c_w = [channel(f"c_w{i}") for i in range(NRAW)]

        class Stream:
            loaded = 0
            split = 0
            used = 0
            raw_free = [[] for _ in range(NRAW)]
            raw_ready = {}
            parts_free = [[] for _ in range(NSPLIT)]
            ready = {}

            def load(self):
                n = self.loaded
                s = n % NRAW
                self.raw_ready[n] = c_w[s].start(sp, wraw[s][:, :], wstream[n], *self.raw_free[s])
                self.loaded += 1

            def part(self):
                n = self.split
                while self.loaded <= n:
                    self.load()
                r, s = n % NRAW, n % NSPLIT
                t1 = act.op(lambda e: e.copy(wh[s][:, :], wraw[r][:, :]), self.raw_ready[n], *self.parts_free[s])
                t2 = pool.op(lambda e: e.tensor_tensor(wl[s][:, :], wraw[r][:, :], wh[s][:, :].bitcast(F32),
                                                       ALU.subtract), t1, *self.parts_free[s])
                self.raw_free[r] = [t1, t2]
                self.ready[n] = (t1, t2)
                self.split += 1
                if self.loaded < min(n + NRAW, N_TILES):
                    self.load()

            def get(self, ahead=0):
                while self.split < min(self.used + NSPLIT, N_TILES):
                    self.part()
                n = self.used + ahead
                return n % NSPLIT, self.ready[n]

            def done(self, token):
                self.parts_free[self.used % NSPLIT] = [token]
                self.used += 1

        ws = Stream()

        c_h = [channel(f"c_h{i}") for i in range(KT)]
        c_gn, c_cst = channel("c_gn"), channel("c_cst")
        t_gn = c_gn.start(sp, gn[:, :], gains)
        ws.load()
        t_h = [c_h[k].start(sp, h[:, k, :], hT[:, k, :]) for k in range(KT)]
        t_cst = c_cst.start(sp, cst[:, :], consts)
        for _ in range(NRAW - 2):
            ws.load()
        for e in (dve, act, pool):
            e.wait(t_gn)
        ws.part()
        def passes(bank, s, xh, xl, a, b, x_ready, ks, shift=0):
            o = bank.t[:, 0:b - a]
            for n, k in enumerate(ks):
                pe.wait(*x_ready[k])
                c = (k + shift) * 128
                w1, w2 = wh[s][:, c:c + 128], wl[s][:, c:c + 128]
                x1, x2 = xh[:, k, a:b], xl[:, k, a:b]
                first, end = n == 0, n == len(ks) - 1
                pe.silent(lambda e, w=w1, x=x1, first=first: e.matmul(o, w, x, start=first, stop=False))
                pe.silent(lambda e, w=w1, x=x2: e.matmul(o, w, x, start=False, stop=False))
                f = lambda e, w=w2, x=x1, end=end: e.matmul(o, w, x, start=False, stop=end)
                if end:
                    return pe.op(f)
                pe.silent(f)

        def gemm(xh, xl, chunks, x_ready):
            s, ready = ws.get()
            pe.wait(*ready)
            bs = [gemm_banks.next() for _ in chunks]
            toks = []
            for (a, b), bank in zip(chunks, bs):
                pe.wait(*bank.free)
                toks.append(passes(bank, s, xh, xl, a, b, x_ready, range(KT)))
            ws.done(toks[-1])
            return bs, toks

        def mm_group(parts, *tokens):
            pe.wait(*tokens)
            for i, (o, l, r) in enumerate(parts):
                f = lambda e, o=o, l=l, r=r, i=i: e.matmul(o, l, r, start=(i == 0), stop=(i == len(parts) - 1))
                if i < len(parts) - 1:
                    pe.silent(f)
            return pe.op(f)

        def token_tiles(n):
            return [(t, min(128, n - t)) for t in range(0, n, 128)]

        class Norm:

            def __init__(self, n, bank, col=0, first=True, acc=None):
                self.acc, self.t_acc, self.flushed = acc, None, False
                self.tts = token_tiles(n)
                self.n, self.bank, self.col, self.first = n, bank, col, first
                self.t_mm = None

            def square(self, src, tok, scale=1.0, rows=128):
                q = sq.next()
                t = act.op(lambda e: e.activation(q.t[0:rows, 0:self.n], src, ACT.Square, scale=scale), tok, *q.free)
                self.due = (q, t, rows)

            def finish(self):
                q, t, rows = self.due
                self.flush(rows)
                q.free = [self.sum(q.t, t, rows, True)]

            def add(self, src, tok, scale=1.0, rows=128, last=False, adder=dve):
                if self.acc and self.t_acc is None:
                    self.t_acc = act.op(lambda e: e.activation(self.acc.t[0:rows, 0:self.n], src, ACT.Square,
                                                               scale=scale), tok, *self.acc.free)
                    return
                q = sq.next()
                t = act.op(lambda e: e.activation(q.t[0:rows, 0:self.n], src, ACT.Square, scale=scale), tok, *q.free)
                if self.acc and not last:
                    self.t_acc = adder.op(lambda e: e.tensor_tensor(self.acc.t[0:rows, 0:self.n],
                                                                  self.acc.t[0:rows, 0:self.n],
                                                                  q.t[0:rows, 0:self.n], ALU.add), t, self.t_acc)
                    q.free = [self.t_acc]
                    return
                self.flush(rows)
                q.free = [self.sum(q.t, t, rows, last)]

            def flush(self, rows=128):
                if self.acc and not self.flushed:
                    self.acc.free = [self.sum(self.acc.t, self.t_acc, rows)]
                    self.flushed = True

            def sum(self, ap, t, rows=128, last=False):
                pe.wait(t)
                if self.t_mm is None:
                    pe.wait(*self.bank.free)
                for j, (a, m) in enumerate(self.tts):
                    f = lambda e, j=j, a=a, m=m, first=self.first, c=self.col: e.matmul(
                        self.bank.t[0:m, c + j:c + j + 1], ap[0:rows, a:a + m], ones[0:rows, 0:1],
                        start=first, stop=last, skip_group_check=True)
                    if j < len(self.tts) - 1:
                        pe.silent(f)
                    self.first = False
                self.t_mm = pe.op(f)
                return self.t_mm

            def scale(self, size, slot=2):
                full = [j for j, (a, m) in enumerate(self.tts) if m == 128]
                parts = [(128, 0, len(full))] + [(m, j, j + 1) for j, (a, m) in enumerate(self.tts) if m < 128]
                for p, a, b in parts:
                    s0, s1, s2 = st[0:p, 0, a:b], st[0:p, 1, a:b], st[0:p, slot, a:b]
                    src = self.bank.t[0:p, self.col + a:self.col + b]
                    t = dve.op(lambda e, s0=s0, src=src: e.tensor_scalar(s0, src, 1.0 / size, EPS, ALU.mult, ALU.add),
                               self.t_mm, st_free[0])
                    self.bank.free = [t]
                    t = act.op(lambda e, s0=s0, s1=s1: e.sqrt(s1, s0), t)
                    t = dve.op(lambda e, s1=s1, s2=s2: e.reciprocal(s2, s1), t)
                return t

        def spread(tts, t, slot, bank, to_psum=False):
            td = [dve.op(lambda e, j=j, m=m: e.tensor_scalar(diag[0:m, j, 0:m], ident[0:m, 0:m],
                                                             st[0:m, slot, j:j + 1], None, ALU.mult), t, diag_free[0])
                  for j, (a, m) in enumerate(tts)]
            pe.wait(*bank.free)
            for j, (a, m) in enumerate(tts):
                t_bc = pe.op(lambda e, j=j, a=a, m=m: e.matmul(bank.t[:, a:a + m], ones[0:m, :], diag[0:m, j, 0:m],
                                                               start=True, stop=True), td[j])
            diag_free[0] = t_bc
            n = tts[-1][0] + tts[-1][1]
            st_free[0] = td[-1]
            if to_psum:
                return t_bc
            t_rb = act.op(lambda e: e.copy(rb[:, 0:n], bank.t[:, 0:n]), t_bc, rb_free[0])
            bank.free = [t_rb]
            return t_rb

        diag_free = [None]

        def warm_sqrt():
            act.op(lambda e: e.sqrt(st[:, 3, 0:1], ones[:, 0:1]))

        def split(src, src_tok, xh, xl, *free, lo=pool):
            t1 = act.op(lambda e: e.copy(xh, src), src_tok, *free)
            t2 = lo.op(lambda e: e.tensor_tensor(xl, src, xh.bitcast(F32), ALU.subtract), t1, src_tok, *free)
            return (t1, t2)

        def scaled_split(src, gain, n, t_rb, tmp, xh, xl, *tokens, lo=pool, by=None):
            b = tmp.next()
            r = rb if by is None else by.t
            t = dve.op(lambda e: e.scalar_tensor_tensor(b.t[:, 0:n], src, gain, r[:, 0:n], ALU.mult, ALU.mult),
                       t_rb, *b.free, *tokens)
            parts_ = split(b.t[:, 0:n], t, xh, xl, lo=lo)
            b.free = list(parts_)
            if by is None:
                rb_free[0] = t
            else:
                by.free = [t]
            return parts_

        def dump(name, ap, *tokens):
            if dbg is not None and name in dbg:
                c = channel("c_dbg_" + name)
                t = c.start(sp, dbg[name], ap, *[e.last() for e in engines], *tokens)
                for e in engines:
                    e.wait(t)

        A = ExitStack()
        c_a = [channel(f"c_a{i}") for i in range(3)]
        trg = sb(A, "trg", [128, T])
        uq = sb(A, "uq", [128, 2048])
        ukv = sb(A, "ukv", [128, 1024])
        cq = sb(A, "cq", [128, 3, T])
        cqn = sb(A, "cqn", [128, 3, T])
        kr = sb(A, "kr", [128, T])
        PADC = 14
        hc = sb(A, "hc", [128, 4, PADC + T])
        vt = sb(A, "vt", [128, 5, 512])
        kTh = Ring([Buf(sb(A, f"kTh{i}", [128, T])) for i in range(2)])
        qTh = Ring([Buf(sb(A, f"qTh{i}", [128, 512])) for i in range(2)])
        Pb = Ring([Buf(sb(A, f"P{i}", [128, T])) for i in range(4)])
        PTb = Ring([Buf(sb(A, f"PT{i}", [128, 640])) for i in range(3)])
        mx = Ring([Buf(sb(A, f"mx{i}", [128, 4])) for i in range(6)])
        attn = sb(A, "attn", [128, 4, 512])
        co = sb(A, "co", [128, 4, 512])

        t_z = pool.op(lambda e: e.memset(hc[:, :, 0:PADC], 0.0))

        x_ready = []
        nx = Norm(T, wide[0], acc=Buf(attn[:, :, :].rearrange("p i t -> p (i t)")))

        def gain_of(k):
            b = tmp.next()
            t = dve.op(lambda e: e.tensor_scalar(b.t[:, :], h[:, k, :], g("g_mix", k), None, ALU.mult), t_h[k], *b.free)
            t1 = act.op(lambda e: e.copy(XH[:, k, :], b.t[:, :]), t)
            return b, t1

        coming = gain_of(0)
        for k in range(KT):
            b, t1 = coming
            if k + 1 < KT:
                coming = gain_of(k + 1)
            t2 = dve.op(lambda e, k=k, b=b: e.tensor_tensor(XL[:, k, :], b.t[:, :], XH[:, k, :].bitcast(F32),
                                                            ALU.subtract), t1)
            b.free = [t1, t2]
            x_ready.append((t1, t2))
            if k < KT - 1:
                nx.add(h[:, k, :], t_h[k], adder=pool)
            else:
                nx.square(h[:, k, :], t_h[k])

        CH = [(0, 264), (264, 528)]
        t_c = []
        outs = []
        for i in range(3):
            outs.append(gemm(XH, XL, CH, x_ready))
            if i == 0:
                t_trg = c_a[0].start(sp, trg[:, :], trig)
                continue
            if i == 1:
                t_uq = c_a[1].start(sp, uq[:, :], w_uq)
                for e in engines:
                    e.wait(t_cst)
                t_b = [act.op(lambda e: e.copy(identb[:, :], ident)), act.op(lambda e: e.copy(cmaskb[:, :], cmask))]
                t_b += [act.op(lambda e: e.mul(inv512[:, :], ones, 1.0 / 512.0)),
                        act.op(lambda e: e.mul(inv64[:, :], ones, 1.0 / 64.0))]
                pe.wait(*t_b)
                nx.finish()
                t_rb = spread(nx.tts, nx.scale(D), 2, wide[1])
            else:
                t_ukv = c_a[2].start(sp, ukv[:, :], w_ukv)
            while outs:
                bs, tk = outs.pop(0)
                j = len(t_c)
                for (a, b), bank, t in zip(CH, bs, tk):
                    te = dve.op(lambda e, j=j, a=a, b=b, bank=bank: e.tensor_tensor(
                        cq[:, j, a:b], bank.t[:, 0:b - a], rb[:, a:b], ALU.mult), t, t_rb)
                    bank.free = [te]
                t_c.append(te)
        bs, tk = gemm(XH, XL, CH, x_ready)
        dve.wait(t_trg)
        for (a, b), bank, t in zip(CH, bs, tk):
            u, v = tmp.next(), tmp.next()
            t = dve.op(lambda e, a=a, b=b, bank=bank, v=v: e.tensor_tensor(v.t[64:128, a:b], bank.t[64:128, 0:b - a],
                                                                           rb[64:128, a:b], ALU.mult), t, *v.free)
            bank.free = [t]
            t1 = dve.op(lambda e, a=a, b=b, v=v: e.tensor_tensor(kr[64:96, a:b], v.t[64:96, a:b],
                                                                 trg[64:96, a:b], ALU.mult), t)
            t2 = dve.op(lambda e, a=a, b=b, v=v, u=u: e.tensor_tensor(u.t[64:96, a:b], v.t[96:128, a:b],
                                                                      trg[96:128, a:b], ALU.mult), t, *u.free)
            v.free = [t2]
            t_kr = dve.op(lambda e, a=a, b=b, u=u: e.tensor_tensor(kr[64:96, a:b], kr[64:96, a:b], u.t[64:96, a:b],
                                                                   ALU.add), t1, t2)
            u.free = [t_kr]
        nq = Norm(T, wide[0], acc=Buf(attn[:, :, :].rearrange("p i t -> p (i t)")))
        nq.acc.free = nx.acc.free
        nq.add(cq[:, 0, :], t_c[0])
        nq.add(cq[:, 1, :], t_c[1], last=True)
        t_q2 = nq.scale(256, slot=2)
        wide[0].free = [t_q2]
        nk = Norm(T, wide[0])
        nk.add(cq[:, 2, :], t_c[2], last=True)
        t_k3 = nk.scale(128, slot=3)

        taps = []
        taps_a = []
        t_co = [None] * 4

        def tap(c, k):
            w = g("conv_w", c * 31 + k)
            x = hc[:, c, k:k + 512]
            if k == 0:
                t_co[c] = dve.op(lambda e: e.tensor_scalar(co[:, c, :], x, w, g("conv_b", c), ALU.mult, ALU.add),
                                 t_hc[c], t_z)
            else:
                t_co[c] = dve.op(lambda e: e.scalar_tensor_tensor(co[:, c, :], x, w, co[:, c, :], ALU.mult, ALU.add),
                                 t_co[c])

        def tap_a(c, k):
            w = g("conv_w", c * 31 + k)
            x = hc[:, c, k:k + 512]
            if k == 0:
                t_co[c] = act.op(lambda e: e.activation(co[:, c, :], x, ACT.Identity, bias=g("conv_b", c), scale=w),
                                 t_hc[c], t_z)
            else:
                b = sq.next()
                t = act.op(lambda e, b=b: e.mul(b.t[:, 0:512], x, w), t_hc[c], *b.free)
                t_co[c] = pool.op(lambda e, b=b: e.tensor_tensor(co[:, c, :], co[:, c, :], b.t[:, 0:512], ALU.add),
                                  t, t_co[c])
                b.free = [t_co[c]]

        def conv_some(n):
            for _ in range(min(n, len(taps))):
                if taps[0] == (2, 16) and (2, 15) in taps_a:
                    return
                tap(*taps.pop(0))

        def conv_a(n):
            for _ in range(min(n, len(taps_a))):
                tap_a(*taps_a.pop(0))

        ktoks = [(0, META)] + [(META + 128 * i, 128) for i in range(4)]
        ukv_v = ukv[:, :].rearrange("p (h e) -> p h e", h=8)[:, :, 64:128]

        SC = 1.0 / (96.0 ** 0.5)
        t_bank, m_bank, x_bank, pair = banks
        q_of, k_of, unit = {}, {}, {}

        def project_q(hd, x_bank=x_bank):
            qb = qTh.next()
            t = mm_group([(x_bank.t[:, 0:512], uq[:, hd * 256 + k * 128:hd * 256 + k * 128 + 128], cqn[:, k, META:T])
                          for k in range(2)], *t_qn, *x_bank.free)
            u, v = tmp.next(), tmp.next()
            t0 = act.op(lambda e: e.mul(qb.t[0:64, :], x_bank.t[0:64, 0:512], SC), t, *qb.free)
            t1 = dve.op(lambda e: e.scalar_tensor_tensor(
                u.t[64:96, 0:512], x_bank.t[64:96, 0:512], SC, trg[64:96, META:T], ALU.mult, ALU.mult), t0, *u.free)
            t2 = dve.op(lambda e: e.scalar_tensor_tensor(
                v.t[64:96, 0:512], x_bank.t[96:128, 0:512], SC, trg[96:128, META:T], ALU.mult, ALU.mult), t, *v.free)
            t3 = dve.op(lambda e: e.tensor_tensor(qb.t[64:96, :], u.t[64:96, 0:512], v.t[64:96, 0:512], ALU.add),
                        t1, t2, *qb.free)
            x_bank.free = [t0, t2]
            u.free = v.free = [t3]
            q_of[hd] = (qb, (t0, t3))

        def project_k(hd, half, x_bank=x_bank):
            if half == 0:
                kb = kTh.next()
                t = dve.op(lambda e: e.tensor_copy(kb.t[64:96, :], kr[64:96, :]), t_kr, *kb.free)
                k_of[hd] = (kb, [t])
            kb, toks = k_of[hd]
            a, b = CH[half]
            t = mm_group([(x_bank.t[0:64, 0:b - a], ukv[:, hd * 128:hd * 128 + 64], cqn[:, 2, a:b])], t_kvn,
                         *x_bank.free)
            t = act.op(lambda e: e.copy(kb.t[0:64, a:b], x_bank.t[0:64, 0:b - a]), t, *kb.free)
            x_bank.free = [t]
            toks.append(t)

        def scores(hd, qt):
            n, d0 = META + 128 * (qt + 1), META + 128 * qt
            qb, tq = q_of[hd]
            kb, tk_ = k_of[hd]
            wb = wide_banks.next()
            pe.wait(*wb.free, *tq, *tk_)
            for a, b in [(0, min(n, 512))] + ([(512, n)] if n > 512 else []):
                pe.silent(lambda e, a=a, b=b: e.matmul(
                    wb.t[:, a:b], qb.t[0:96, qt * 128:qt * 128 + 128], kb.t[0:96, a:b], start=True, stop=False,
                    skip_group_check=True))
                da, db = max(a, d0), min(b, n)
                tS = pe.op(lambda e, da=da, db=db: e.matmul(
                    wb.t[:, da:db], identb[:, :], cmaskb[:, da - d0:db - d0], start=False, stop=True,
                    skip_group_check=True))
            if qt == 3:
                qb.free = [tS]
                kb.free = [tS]
            unit[hd, qt] = (wb, tS)

        def soften(hd, qt):
            n = META + 128 * (qt + 1)
            wb, tS = unit[hd, qt]
            m, P = mx.next(), Pb.next()
            t6 = dve.op(lambda e: e.tensor_reduce(m.t[:, 0:1], wb.t[:, 0:n], AX.X, ALU.max, negate=True), tS, *m.free)
            t7 = act.op(lambda e: e.activation(P.t[:, 0:n], wb.t[:, 0:n], ACT.Exp, bias=m.t[:, 0:1],
                                               accum_out=m.t[:, 1:2]), t6, *P.free)
            wb.free = [t7]
            unit[hd, qt] = (P, m, t7)

        def normalize(hd, qt):
            n = META + 128 * (qt + 1)
            P, m, t7 = unit[hd, qt]
            conv_some(1)
            conv_a(1)
            t8 = dve.op(lambda e: e.reciprocal(m.t[:, 2:3], m.t[:, 1:2]), t7)
            conv_some(1)
            conv_a(1)
            t9 = dve.op(lambda e: e.tensor_scalar(P.t[:, 0:n], P.t[:, 0:n], m.t[:, 2:3], None, ALU.mult), t8)
            m.free = [t9]
            unit[hd, qt] = (P, t9)

        def turn(hd, qt):
            P, t9 = unit[hd, qt]
            pt = PTb.next()
            pe.wait(t9, *t_bank.free, *m_bank.free)
            pe.silent(lambda e: e.transpose(m_bank.t[0:META, 0:128], P.t[:, 0:META], ident))
            for i in range(qt + 1):
                f = lambda e, i=i: e.transpose(
                    t_bank.t[:, i * 128:i * 128 + 128], P.t[:, META + i * 128:META + i * 128 + 128], ident)
                if i < qt:
                    pe.silent(f)
            tT = pe.op(f)
            P.free = [tT]
            ta_ = act.op(lambda e: e.copy(pt.t[0:META, 512:640], m_bank.t[0:META, 0:128]), tT, *pt.free)
            tb_ = act.op(lambda e: e.copy(pt.t[:, 0:128 * (qt + 1)], t_bank.t[:, 0:128 * (qt + 1)]), tT, *pt.free)
            t_bank.free, m_bank.free = [tb_], [ta_]
            unit[hd, qt] = (pt, (ta_, tb_))

        def values(hd, qt):
            pt, toks = unit.pop((hd, qt))
            b0 = 64 * (hd % 2)
            if hd % 2 == 0 and qt == 0:
                pe.wait(*pair.free)
            pe.wait(*toks, t_v)
            o = pair.t[b0:b0 + 64, qt * 128:qt * 128 + 128]
            pe.silent(lambda e: e.matmul(o, vt[0:META, 0, hd * 64:hd * 64 + 64], pt.t[0:META, 512:640],
                                         start=True, stop=False, skip_group_check=True))
            for i in range(qt + 1):
                f = lambda e, i=i: e.matmul(o, vt[:, 1 + i, hd * 64:hd * 64 + 64], pt.t[:, i * 128:i * 128 + 128],
                                            start=False, stop=(i == qt), skip_group_check=True)
                if i < qt:
                    pe.silent(f)
            tO = pe.op(f)
            pt.free = [tO]
            if hd % 2 == 1 and qt == 3:
                t_at.append(act.op(lambda e: e.copy(attn[:, hd // 2, :], pair.t[:, :]), tO))
                pair.free = [t_at[-1]]

        t_hc = []
        for c in range(4):
            bsa, ta = gemm(XH, XL, CH, x_ready)
            if c == 0:
                t = spread(nq.tts, t_q2, 2, wide[1], to_psum=True)
                t_qn = [dve.op(lambda e, i=i: e.scalar_tensor_tensor(cqn[:, i, :], cq[:, i, :], g("g_q", i),
                                                                     wide[1].t[:, 0:T], ALU.mult, ALU.mult), t)
                        for i in range(2)]
                wide[1].free = [t_qn[1]]
            v = tmp.next()
            for i, (a, b) in enumerate(CH):
                tv_ = dve.op(lambda e, a=a, b=b, v=v, bank=bsa[i]: e.tensor_tensor(
                    v.t[:, a:b], bank.t[:, 0:b - a], rb[:, a:b], ALU.mult), ta[i], *v.free)
                bsa[i].free = [tv_]
            if c > 0:
                conv_some(8 if c < 3 else 3)
                conv_a(5)
            if c == 3:
                scores(0, 0)
                scores(0, 1)
                soften(0, 0)
                soften(0, 1)
                normalize(0, 0)
            bsb, tb = gemm(XH, XL, CH, x_ready)
            if c == 0:
                t = spread(nk.tts, t_k3, 3, wide[0], to_psum=True)
                t_kvn = dve.op(lambda e: e.scalar_tensor_tensor(cqn[:, 2, :], cq[:, 2, :], g("g_kv"),
                                                                wide[0].t[:, 0:T], ALU.mult, ALU.mult), t)
                wide[0].free = [t_kvn]
            u = tmp.next()
            for i, (a, b) in enumerate(CH):
                tu = dve.op(lambda e, a=a, b=b, u=u, bank=bsb[i]: e.tensor_tensor(
                    u.t[:, a:b], bank.t[:, 0:b - a], rb[:, a:b], ALU.mult), tb[i], *u.free)
                bsb[i].free = [tu]
                ts = act.op(lambda e, a=a, b=b, u=u: e.activation(u.t[:, a:b], u.t[:, a:b], ACT.Sigmoid), tu)
                tm = dve.op(lambda e, a=a, b=b, u=u, v=v, c=c: e.tensor_tensor(
                    hc[:, c, PADC + a:PADC + b], v.t[:, a:b], u.t[:, a:b], ALU.mult), ts)
            u.free = v.free = [tm]
            t_hc.append(tm)
            taps.extend((c, k) for k in range(31) if c < 2 or c == 2 and k >= 16)
            taps_a.extend((c, k) for k in range(31) if c == 3 or c == 2 and k < 16)
            conv_some(3)
            if c == 2:
                project_q(0, wide[0])
                project_k(0, 0, wide[1])
                project_k(0, 1, wide[1])
            if c == 1:
                pe.wait(t_uq, t_ukv)
                for i, (a, m) in enumerate(ktoks):
                    bank = gemm_banks.next()
                    t = mm_group([(bank.t[0:m, :], cqn[:, 2, a:a + m], ukv_v)], t_kvn, *bank.free)
                    t_v = act.op(lambda e, i=i, m=m, bank=bank: e.copy(vt[0:m, i, :], bank.t[0:m, :]), t)
                    bank.free = [t_v]
        rb_free[0] = tu
        dump("hc", hc[:, :, PADC:])

        t_at = []
        cv_ready = []
        conv_bank = [x_bank]

        def conv_norms():
            cb = conv_bank[0]
            pe.wait(*t_co, *cb.free)
            b = mm_group([(cb.t[:, :], inv512[:, :], co[:, c, :]) for c in range(4)], *t_co)
            for c in range(4):
                t_co[c] = dve.op(lambda e, c=c: e.tensor_tensor(co[:, c, :], co[:, c, :], cb.t[:, :],
                                                                ALU.subtract), b)
            cb.free = [t_co[3]]
            yield
            toks = t_co
            acc = Buf(cq[:, 1, :])
            for last in (False, True):
                nc_ = Norm(512, conv_bank[0], acc=acc)
                for c in range(3):
                    nc_.add(co[:, c, :], toks[c])
                nc_.square(co[:, 3, :], toks[3])
                yield
                nc_.finish()
                t = nc_.scale(512)
                yield
                t_rb = spread(nc_.tts, t, 2, conv_bank[0])
                yield
                if not last:
                    toks = []
                    for c in range(4):
                        t1 = dve.op(lambda e, c=c: e.scalar_tensor_tensor(
                            co[:, c, :], co[:, c, :], g("g_ln", c), rb[:, 0:512], ALU.mult, ALU.mult), t_rb)
                        rb_free[0] = t1
                        toks.append(act.op(lambda e, c=c: e.activation(co[:, c, :], co[:, c, :], ACT.Silu,
                                                                       bias=g("b_ln", c)), t1))
                    yield
            for c in range(4):
                cv_ready.append(scaled_split(co[:, c, :], g("g_oc", c), 512, t_rb, either, XH[:, 4 + c, 0:512],
                                             XL[:, 4 + c, 0:512], xin_used, lo=(pool, dve)[c % 2]))

        conv_steps = conv_norms()
        xin_used = pe.last()
        units = [(hd, qt) for hd in range(8) for qt in range(4)]
        na = Norm(512, wide[0], acc=Buf(cq[:, 0, :]))
        for n in range(len(units) + 4):
            if n < len(units):
                hd, qt = units[n]
                if n > 1:
                    scores(hd, qt)
            if 0 <= n - 3 < len(units):
                turn(*units[n - 3])
            if n < len(units):
                if n > 1:
                    soften(hd, qt)
                if hd + 1 < 8:
                    if qt == 0:
                        project_q(hd + 1)
                    elif qt < 3:
                        project_k(hd + 1, qt - 1)
            if 1 < n <= len(units):
                normalize(*units[n - 1])
            if 0 <= n - 4 < len(units):
                values(*units[n - 4])
                if units[n - 4] in ((1, 3), (3, 3), (5, 3)):
                    na.add(attn[:, units[n - 4][0] // 2, :], t_at[-1])
            if 31 <= n < 35 and not taps and not taps_a:
                next(conv_steps, None)
        dump("attn", attn[:, :, :])
        na.add(attn[:, 3, :], t_at[3], last=True)
        t_a2 = na.scale(512, slot=3)
        conv_bank[0] = Buf(wide[0].t[:, 0:512])
        conv_bank[0].free = wide[0].free
        FULL = [(0, 512)]
        t_rb = spread(na.tts, t_a2, 3, wide[1], to_psum=True)
        mix_ready = [scaled_split(attn[:, i, :], g("g_oa", i), 512, t_rb, either, XH[:, i, 0:512], XL[:, i, 0:512],
                                  xin_used, lo=(pool, dve)[i % 2], by=wide[1]) for i in range(4)]

        def half_out(half, m):
            s_, ready = ws.get()
            bank = gemm_banks.next()
            pe.wait(*ready, *bank.free)
            t = passes(bank, s_, XH, XL, 0, 512, mix_ready, range(4 * half, 4 * half + 4), 4 * (m % 2 - half))
            if m % 2:
                ws.done(t)
            if half and m > 0:
                nf.add(h[:, m - 1, META:T], t_hk[m - 1])
            if half and m == 7:
                warm_sqrt()
            tt = dve.op(lambda e: e.tensor_tensor(h[:, m, META:T], bank.t[:, :], h[:, m, META:T], ALU.add), t,
                        t_hk[m])
            bank.free = [tt]
            t_hk[m] = tt

        t_hk = [None] * 8
        for m in range(8):
            half_out(0, m)
            next(conv_steps, None)
        for _ in conv_steps:
            pass
        mix_ready += cv_ready
        wide[0].free = conv_bank[0].free
        nf = Norm(512, wide[0], acc=tmp.next())
        for m in range(8):
            half_out(1, m)
        nf.add(h[:, 7, META:T], t_hk[7], last=True)
        t_rb = spread(nf.tts, nf.scale(D), 2, wide[1], to_psum=True)
        dump("h1", h[:, :, META:])
        fence()
        A.close()

        B = ExitStack()
        c_b = channel("c_b")
        ky = sb(B, "ky", [128, 8, 128])
        t_ky = c_b.start(sp, ky[:, :, :], keys)
        qp = sb(B, "qp", [128, 8, 512])
        sv = sb(B, "sv", [128, 16, 16])
        siu = sb(B, "siu", [128, 16, 16], U32)
        sif = sb(B, "sif", [128, 16, 16])
        left = sb(B, "left", [128, 8, 128])
        cand = sb(B, "cand", [128, 8, 256])
        left2 = sb(B, "left2", [128, 8, 256])
        hot = left2[:, :, :].rearrange("p h (k a) -> p (h k) a", a=16)
        tv = sb(B, "tv", [128, 8, 16])
        sel = sb(B, "sel", [128, 8, 16], U32)
        selu = sb(B, "selu", [128, 2, 128], U32)
        self_ = sb(B, "self", [128, 2, 128])
        ijg = sb(B, "ijg", [128, 3, 128])
        sm = sb(B, "sm", [128, 2, 8])
        ijgT = sb(B, "ijgT", [128, 3, 512])
        gs = Ring([Buf(sb(B, f"gs{i}", [128, 128, 32])) for i in range(2)])
        oneA = Ring([Buf(sb(B, f"oneA{i}", [128, 128])) for i in range(8)])
        oneB = Ring([Buf(sb(B, f"oneB{i}", [128, 128])) for i in range(8)])
        c_gs = [channel(f"c_gs{i}") for i in range(2)]
        ge = Ring(tmp.bufs + sq.bufs)
        c_sp = [channel(f"c_sp{i}") for i in range(5)]

        xf_ready = [scaled_split(h[:, k, META:T], g("g_ffn", k), 512, t_rb, either, XH[:, k, 0:512], XL[:, k, 0:512],
                                 pe.last(), lo=dve if k % 3 == 1 else pool, by=wide[1]) for k in range(KT)]
        t_qp = []
        for m in range(8):
            (bank,), (t,) = gemm(XH, XL, FULL, xf_ready)
            te = act.op(lambda e, m=m, bank=bank: e.copy(qp[:, m, :], bank.t[:, :]), t)
            bank.free = [te]
            t_qp.append(te)

        s_bufs = [Ring([Buf(w.t[:, 0:512]), Buf(w.t[:, 512:1024])]) for w in wide]
        t_route = [None] * 4
        ijg_free = [None]
        t_g = []

        def route(tt):
            q0 = tt * 128
            t_i = None
            for half in range(2):
                bp = s_bufs[half].bufs
                for p in range(2):
                    pe.wait(*bp[p].free, *t_qp, t_ky)
                    for i in range(4):
                        hd = half * 4 + i
                        t = pe.op(lambda e, p=p, i=i, hd=hd, bp=bp: e.matmul(
                            bp[p].t[:, i * 128:i * 128 + 128], qp[64 * p:64 * p + 64, hd, q0:q0 + 128],
                            ky[64 * p:64 * p + 64, hd, :], start=True, stop=True, skip_group_check=True))
                units = [(p, i, 2 * (half * 4 + i) + p) for i in range(4) for p in range(2)]
                yield
                dve.wait(t)
                w = [dve.op(lambda e, p=p, i=i, u=u, bp=bp: e.max(sv[:, u, 0:8], bp[p].t[:, i * 128:i * 128 + 128]))
                     for p, i, u in units]
                yield
                for j, (p, i, u) in enumerate(units):
                    dve.op(lambda e, p=p, i=i, u=u, bp=bp: e.max_index(siu[:, u, 0:8], sv[:, u, 0:8],
                                                                       bp[p].t[:, i * 128:i * 128 + 128]), w[j])
                yield
                x = [dve.op(lambda e, p=p, i=i, u=u, j=j, bp=bp: e.match_replace(
                    left[:, j, :], sv[:, u, 0:8], bp[p].t[:, i * 128:i * 128 + 128], TAKEN), w[j])
                    for j, (p, i, u) in enumerate(units)]
                bp[0].free = bp[1].free = [x[-1]]
                yield
                w = [dve.op(lambda e, u=u, j=j: e.max(sv[:, u, 8:16], left[:, j, :]), x[j])
                     for j, (p, i, u) in enumerate(units)]
                yield
                for j, (p, i, u) in enumerate(units):
                    t_i = dve.op(lambda e, u=u, j=j: e.max_index(siu[:, u, 8:16], sv[:, u, 8:16], left[:, j, :]), w[j])
            yield
            t_f = dve.op(lambda e: e.tensor_copy(sif[:, :, :], siu[:, :, :]), t_i)
            s4 = sv[:, :, :].rearrange("p (h q) a -> p h q a", q=2)
            t_cd = dve.op(lambda e: e.tensor_tensor(
                cand[:, :, :].rearrange("p h (a b) -> p h a b", a=16),
                s4[:, :, 0, :].unsqueeze(3).to_broadcast([128, 8, 16, 16]),
                s4[:, :, 1, :].unsqueeze(2).to_broadcast([128, 8, 16, 16]), ALU.add), t_i)
            yield
            w = [dve.op(lambda e, i=i: e.max(tv[:, i, 0:8], cand[:, i, :]), t_cd) for i in range(8)]
            yield
            for i in range(8):
                dve.op(lambda e, i=i: e.max_index(sel[:, i, 0:8], tv[:, i, 0:8], cand[:, i, :]), w[i])
            yield
            x = [dve.op(lambda e, i=i: e.match_replace(left2[:, i, :], tv[:, i, 0:8], cand[:, i, :], TAKEN), w[i])
                 for i in range(8)]
            yield
            w = [dve.op(lambda e, i=i: e.max(tv[:, i, 8:16], left2[:, i, :]), x[i]) for i in range(8)]
            yield
            for i in range(8):
                t_s = dve.op(lambda e, i=i: e.max_index(sel[:, i, 8:16], tv[:, i, 8:16], left2[:, i, :]), w[i])
            yield
            sf = sel[:, :, :].rearrange("p h k -> p (h k)")
            dve.op(lambda e: e.tensor_scalar(selu[:, 0, :], sf, 4, None, ALU.logical_shift_right), t_s)
            t = dve.op(lambda e: e.tensor_scalar(selu[:, 1, :], sf, 15, None, ALU.bitwise_and))
            t = dve.op(lambda e: e.tensor_copy(self_[:, :, :], selu[:, :, :]), t)
            si4 = sif[:, :, :].rearrange("p (h q) a -> p h q a", q=2)
            gv = ijg[:, 2, :].rearrange("p (h k) -> p h k", h=8)
            t2 = dve.op(lambda e: e.tensor_tensor(gv, tv[:, :, :], tv[:, :, 0:1].to_broadcast([128, 8, 16]),
                                                  ALU.subtract), t_s, ijg_free[0])
            t2 = act.op(lambda e: e.activation(gv, gv, ACT.Exp), t2)
            for q in range(2):
                t = dve.op(lambda e, q=q: e.tensor_tensor(
                    hot, self_[:, q, :].unsqueeze(2).to_broadcast([128, 128, 16]),
                    iota[:, 0:16].unsqueeze(1).to_broadcast([128, 128, 16]), ALU.is_equal), t)
                yield
                hv = left2[:, :, :].rearrange("p h (k a) -> p h k a", a=16)
                t = dve.op(lambda e, q=q, hv=hv: e.tensor_tensor(
                    hv, hv, si4[:, :, q, :].unsqueeze(2).to_broadcast([128, 8, 16, 16]), ALU.mult), t, t_f)
                yield
                t = dve.op(lambda e, q=q: e.tensor_reduce(ijg[:, q, :], hot, AX.X, ALU.add), t, ijg_free[0])
                yield
            t2 = dve.op(lambda e: e.tensor_reduce(sm[:, 0, :], gv, AX.X, ALU.add), t2)
            t2 = dve.op(lambda e: e.reciprocal(sm[:, 1, :], sm[:, 0, :]), t2)
            t2 = dve.op(lambda e: e.tensor_tensor(gv, gv, sm[:, 1, :].unsqueeze(2).to_broadcast([128, 8, 16]),
                                                  ALU.mult), t2)
            yield
            yield
            bank = gemm_banks.next()
            pe.wait(t, t2, *bank.free)
            for i in range(3):
                tp = pe.op(lambda e, i=i, bank=bank: e.transpose(bank.t[:, i * 128:i * 128 + 128], ijg[:, i, :],
                                                                 ident))
            ijg_free[0] = tp
            t = act.op(lambda e, bank=bank: e.copy(
                ijgT[:, :, q0:q0 + 128], bank.t[:, 0:384].rearrange("p (i t) -> p i t", i=3)), tp)
            bank.free = [t]
            t_route[tt] = t

        STEPS = 26
        gbuf_of = {}

        def scatter(t0, t_r):
            blk = t0 // 32
            if t0 % 32 == 0:
                gbuf_of[blk] = gs.next()
            gbuf = gbuf_of[blk]
            for q in range(t0 % 32 // 4, t0 % 32 // 4 + 2):
                bank = gemm_banks.next()
                for i in range(4):
                    t = blk * 32 + q * 4 + i
                    a, b = oneA.next(), oneB.next()
                    ta = dve.op(lambda e, a=a, t=t: e.tensor_scalar(a.t[:, :], iota, ijgT[:, 0, t:t + 1],
                                                                    ijgT[:, 2, t:t + 1], ALU.is_equal, ALU.mult),
                                t_r, *a.free)
                    eng = dve if i % 2 else pool
                    tb = eng.op(lambda e, b=b, t=t: e.tensor_scalar(b.t[:, :], iota, ijgT[:, 1, t:t + 1], None,
                                                                    ALU.is_equal), t_r, *b.free)
                    pe.wait(*bank.free)
                    tm = pe.op(lambda e, a=a, b=b, i=i, bank=bank: e.matmul(
                        bank.t[:, i * 128:i * 128 + 128], b.t[:, :], a.t[:, :], start=True, stop=True,
                        skip_group_check=True), ta, tb)
                    a.free = b.free = [tm]
                te = act.op(lambda e, q=q, bank=bank, gbuf=gbuf: e.copy(
                    gbuf.t[:, :, q * 4:q * 4 + 4].rearrange("p i t -> p t i"),
                    bank.t[:, :].rearrange("p (t i) -> p t i", t=4)), tm, *gbuf.free)
                bank.free = [te]
            if t0 % 32 == 24:
                t = c_gs[blk % 2].start(sp, gdram[:, blk, :, :], gbuf.t[:, :, :], te)
                gbuf.free = [t]
                t_g.append(t)

        spilled = [0]
        t_a = []

        def spill():
            n = spilled[0]
            spilled[0] += 1
            (bank,), (t,) = gemm(XH, XL, FULL, xf_ready)
            b = ge.next()
            t1 = act.op(lambda e: e.activation(b.t[:, 0:512], bank.t[:, :], ACT.Gelu), t, *b.free)
            bank.free = [t1]
            t2 = c_sp[n % 5].start(sp, adram[:, n, :], b.t[:, 0:512], t1)
            b.free = [t2]
            t_a.append(t2)

        steps = route(0)
        for n in range(13):
            for _ in range(2):
                next(steps, None)
            spill()
        for _ in steps:
            pass
        for tt in range(4):
            steps = route(tt + 1) if tt < 3 else iter(())
            done = 0
            for n in range(16):
                if spilled[0] < 13 + 59 * (tt * 16 + n + 1) // 64:
                    spill()
                scatter(tt * 128 + n * 8, t_route[tt])
                while done < STEPS * (n + 1) // 16:
                    next(steps, None)
                    done += 1
            for _ in steps:
                pass
        for w, r_ in zip(wide, s_bufs):
            w.free = r_.bufs[0].free
        dump("ijgT", ijgT[:, :, :])
        over = [e.last() for e in engines] + t_g[-2:] + t_a[-5:]
        B.close()

        C = ExitStack()
        WTH = [sb(C, f"WTH{i}", [128, 8, 512], F32R) for i in range(2)]
        WTL = [sb(C, f"WTL{i}", [128, 8, 512], F32R) for i in range(2)]
        gr = Ring([Buf(sb(C, f"gr{i}", [128, 16, 8 * 32])) for i in range(2)])
        c_gr = [channel(f"c_gr{i}") for i in range(3)]
        c_ge = [channel(f"c_ge{i}") for i in range(5)]
        wt_free = [over, over]
        ge = Ring(ge.bufs)
        for b in gr.bufs:
            b.free = over
        wt_ready = [None, None]

        def load_group(n):
            b = gr.next()
            toks = []
            for a in ((0, 4) if n == 0 else (0,)):
                w = 4 if n == 0 else 8
                i0 = ORDER[n] * 8 + a
                c = c_gr[2 if a else n % 2]
                toks += [c.start(sp, b.t[:, :, a * 32:(a + w) * 32], gdram[:, :, i0:i0 + w, :]
                                 .rearrange("p b i t -> p b (i t)"), *b.free)] * w
            return b, toks

        ahead = []
        n_ahead = [0]

        def load_spilled(upto):
            while n_ahead[0] < min(upto, SPILLED * 8):
                slot = ge.at % 5
                b = ge.next()
                ahead.append((b, c_ge[slot].start(sp, b.t[:, 0:512], adram[:, n_ahead[0], :], *b.free)))
                n_ahead[0] += 1

        nxt = [load_group(0)]

        def prepare(n, i):
            gi, s = ORDER[n], n % 2
            if i == 0:
                cur[0] = nxt[0]
                wt_ready[s] = []
            gbuf, t_gr = cur[0][0], cur[0][1][i]
            if gi < SPILLED:
                load_spilled(gi * 8 + i + 3)
                b, t1 = ahead.pop(0)
            else:
                (bank,), (t,) = gemm(XH, XL, FULL, xf_ready)
                b = ge.next()
                t1 = act.op(lambda e: e.activation(b.t[:, 0:512], bank.t[:, :], ACT.Gelu), t, *b.free)
                bank.free = [t1]
            if i == 0 and n + 1 < N_GROUPS:
                nxt[0] = load_group(n + 1)
            t2 = dve.op(lambda e: e.tensor_tensor(
                b.t[:, 0:512].rearrange("p (b t) -> p b t", t=32), b.t[:, 0:512].rearrange("p (b t) -> p b t", t=32),
                gbuf.t[:, :, i * 32:i * 32 + 32], ALU.mult), t1, t_gr)
            t3 = act.op(lambda e: e.copy(WTH[s][:, i, :], b.t[:, 0:512]), t2, *wt_free[s])
            t4 = (pool if n == 0 and i % 2 else dve).op(lambda e: e.tensor_tensor(WTL[s][:, i, :], b.t[:, 0:512], WTH[s][:, i, :].bitcast(F32),
                                                  ALU.subtract), t3, *wt_free[s])
            b.free = [t3, t4]
            wt_ready[s].append((t3, t4))
            gbuf.free = [t2]

        def combine(n, m):
            s = n % 2
            (bank,), (t,) = gemm(WTH[s], WTL[s], FULL, wt_ready[s])
            if n == N_GROUPS - 1 and m > 0:
                if m == 7:
                    warm_sqrt()
                square_of(m - 1)
            t_hk[m] = dve.op(lambda e: e.tensor_tensor(h[:, m, META:T], bank.t[:, :], h[:, m, META:T], ALU.add),
                             t, t_hk[m])
            bank.free = [t_hk[m]]
            if m == 7:
                wt_free[s] = [t]

        cur = [None]
        hx = [h[:, k, META:T] for k in range(KT)]
        gg = st_gg[:, :]
        t_gg = dve.op(lambda e: e.tensor_tensor(gg, gn[:, GCOL["g_fin"]:GCOL["g_fin"] + 8],
                                                gn[:, GCOL["g2"]:GCOL["g2"] + 8], ALU.mult))
        n1, n2 = Norm(512, wide[0], acc=tmp.bufs[0]), Norm(512, wide[0], col=8, first=False, acc=tmp.bufs[1])

        def square_of(m):
            n1.add(hx[m], t_hk[m], last=(m == 7))
            n2.add(hx[m], t_hk[m], scale=g("g_fin", m), last=(m == 7))

        for what, n, i in expert_steps():
            (prepare if what == "U" else combine)(n, i)
        n1.flush()
        n2.flush()
        square_of(7)
        c1, c2 = wide[0].t[:, 0:4], wide[0].t[:, 8:12]
        t = dve.op(lambda e: e.tensor_scalar(st[:, 2, 0:4], c1, 1.0 / D, EPS, ALU.mult, ALU.add), n2.t_mm, st_free[0])
        t2 = dve.op(lambda e: e.tensor_scalar(st[:, 0, 0:4], c2, 1.0 / D, None, ALU.mult))
        wide[0].free = [t2]
        t = dve.op(lambda e: e.scalar_tensor_tensor(st[:, 0, 0:4], st[:, 2, 0:4], EPS, st[:, 0, 0:4], ALU.mult,
                                                    ALU.add), t, t2)
        t = act.op(lambda e: e.sqrt(st[:, 1, 0:4], st[:, 0, 0:4]), t)
        t1 = act.op(lambda e: e.sqrt(st[:, 2, 0:4], st[:, 2, 0:4]))
        t = dve.op(lambda e: e.reciprocal(st[:, 0, 0:4], st[:, 1, 0:4]), t)
        t_bc = spread(n1.tts, t, 0, wide[1], to_psum=True)
        t_r1 = dve.op(lambda e: e.reciprocal(st[:, 2, 0:4], st[:, 2, 0:4]), t1)
        dump("h2", h[:, :, META:])
        over = [e.last() for e in engines]
        C.close()

        E = ExitStack()
        mixed = sb(E, "mixed", [128, 8, 512])
        ckvT = sb(E, "ckvT", [128, 512])
        ckv = sb(E, "ckv", [128, 4, 128])
        dt_ = [sb(E, f"dt{i}", [128, 128 * (i + 1)]) for i in range(1, 4)]
        uv = sb(E, "uv", [128, 16, 64])
        c_e = [channel(f"c_e{i}") for i in range(3)]
        x2_ready = [scaled_split(hx[k], gg[:, k:k + 1], 512, t_bc, either, XH[:, k, 0:512], XL[:, k, 0:512], t_gg,
                                 lo=dve if k % 3 == 1 else pool, by=wide[1]) for k in range(KT)]
        for e in (dve, act, pool, sp):
            e.wait(*over)
        t_uv = c_e[0].start(sp, uv[:, :, :], w_uv)

        R = ExitStack()
        hgh = sb(R, "hgh", [128, 8, 512], F32R)
        hgl = sb(R, "hgl", [128, 8, 512], F32R)
        wx = sb(R, "wx", [128, 4, 8])
        rg = sb(R, "rg", [128, 2, 8, 128])
        t_rg = c_e[1].start(sp, rg[:, :, :, :], w_rg)
        sidx = [sb(R, f"sidx{i}", [128, 128 * (i + 1)]) for i in range(1, 4)]
        top8 = Ring([Buf(sb(R, f"top8_{i}", [128, 8])) for i in range(6)])
        rt = [Buf(sb(R, f"rt{i}", [128, 515])) for i in range(4)]
        sps = sb(R, "sps", [128, 8, 8])
        Q = ExitStack()
        qi = sb(Q, "qi", [128, 4, 512])
        kx = sb(Q, "kx", [128, 512])

        (bank,), (t,) = gemm(XH, XL, FULL, x2_ready)
        te = act.op(lambda e, bank=bank: e.copy(kx[0:96, :], bank.t[0:96, :]), t)
        bank.free = [te]
        u = tmp.next()
        tw = dve.op(lambda e, u=u: e.tensor_scalar(u.t[64:96, 0:512], kx[64:96, :], 8.0 ** -0.5, None, ALU.mult), te,
                    *u.free)
        t_qi = []

        def index_q(i):
            (bank,), (t,) = gemm(XH, XL, FULL, x2_ready)
            te = act.op(lambda e: e.mul(qi[:, i, :], bank.t[:, :], 0.125), t)
            bank.free = [te]
            t_qi.append(te)

        index_q(0)
        bank = gemm_banks.next()
        pe.wait(tw, *bank.free)
        for j in range(4):
            t = pe.op(lambda e, j=j, u=u, bank=bank: e.matmul(
                bank.t[:, j * 8:j * 8 + 8], u.t[64:96, j * 128:j * 128 + 128], ident[64:96, 64:72],
                start=True, stop=True, skip_group_check=True))
        t_wx = act.op(lambda e, bank=bank: e.copy(wx[:, :, :], bank.t[:, 0:32].rearrange("p (j w) -> p j w", w=8)), t)
        bank.free = [t_wx]
        u.free = [t]
        bank = gemm_banks.next()
        t = mm_group([(bank.t[:, :], inv64[0:64, :], kx[0:64, :])], te, *bank.free)
        t_kc = dve.op(lambda e, bank=bank: e.tensor_tensor(kx[0:64, :], kx[0:64, :], bank.t[0:64, :], ALU.subtract), t)
        bank.free = [t_kc]
        index_q(1)
        ni = Norm(512, wide[1])
        ni.add(kx[0:64, :], t_kc, rows=64, last=True)
        t_ni = ni.scale(64, slot=3)
        t_bc = spread(n1.tts, t_r1, 2, wide[0], to_psum=True)
        for k in range(KT):
            t_hk[k] = dve.op(lambda e, k=k: e.scalar_tensor_tensor(
                hx[k], hx[k], g("g_fin", k), wide[0].t[:, 0:512], ALU.mult, ALU.mult), t_bc)
        wide[0].free = [t_hk[-1]]
        dump("x2", h[:, :, META:])
        index_q(2)
        t_bc = spread(ni.tts, t_ni, 3, wide[1], to_psum=True)
        t = dve.op(lambda e: e.scalar_tensor_tensor(kx[0:64, :], kx[0:64, :], gn[0:64, GCOL["g_idx"]:GCOL["g_idx"] + 1],
                                                    wide[1].t[0:64, 0:512], ALU.mult, ALU.mult), t_bc)
        wide[1].free = [t]
        t = dve.op(lambda e: e.tensor_scalar(kx[0:64, :], kx[0:64, :], gn[0:64, GCOL["b_idx"]:GCOL["b_idx"] + 1], None,
                                             ALU.add), t)
        t_kx = act.op(lambda e: e.copy(kx[64:128, :], kx[0:64, :]), t, tw)
        index_q(3)
        dump("kx", kx[:, :])
        (bank,), (t,) = gemm(XH, XL, FULL, x2_ready)
        t_cv = act.op(lambda e, bank=bank: e.copy(ckvT[:, :], bank.t[:, :]), t)
        bank.free = [t_cv]

        def latent_keys():
            nv = Norm(512, wide[1])
            nv.add(ckvT[:, :], t_cv, last=True)
            t = nv.scale(128)
            yield
            t = spread(nv.tts, t, 2, wide[1], to_psum=True)
            t_ct = dve.op(lambda e: e.scalar_tensor_tensor(ckvT[:, :], ckvT[:, :], g("g_kv2"), wide[1].t[:, 0:512],
                                                           ALU.mult, ALU.mult), t)
            wide[1].free = [t_ct]
            yield
            bank = gemm_banks.next()
            pe.wait(t_ct, *bank.free)
            for j in range(4):
                t = pe.op(lambda e, j=j, bank=bank: e.transpose(bank.t[:, j * 128:j * 128 + 128],
                                                                ckvT[:, j * 128:j * 128 + 128], ident))
            t_ck = act.op(lambda e: e.copy(ckv[:, :, :], bank.t[:, :].rearrange("p (j c) -> p j c", c=128)), t)
            bank.free = [t_ck]
            latent.extend([t_ct, t_ck])

        latent = []
        latent_steps = latent_keys()

        t_si = [None] * 3
        for j in range(8):
            if j % 2:
                next(latent_steps, None)
            p0 = 64 * (j % 2)
            for qt in range(1, 4):
                n = 128 * (qt + 1)
                bank = gemm_banks.next()
                t = mm_group([(bank.t[:, 0:n], qi[p0:p0 + 64, j // 2, qt * 128:qt * 128 + 128], kx[p0:p0 + 64, 0:n])],
                             t_kx, *t_qi, *bank.free)
                u = tmp.next()
                tr = act.op(lambda e, u=u, bank=bank, n=n: e.activation(u.t[:, 0:n], bank.t[:, 0:n], ACT.Relu), t,
                            *u.free)
                bank.free = [tr]
                so = sidx[qt - 1][:, :]
                if j == 0:
                    ta = dve.op(lambda e, u=u, so=so, n=n, qt=qt: e.tensor_scalar(so, u.t[:, 0:n], wx[:, qt, 0:1],
                                                                                  None, ALU.mult), tr, t_wx)
                else:
                    ta = dve.op(lambda e, u=u, so=so, n=n, qt=qt, j=j: e.scalar_tensor_tensor(
                        so, u.t[:, 0:n], wx[:, qt, j:j + 1], so, ALU.mult, ALU.add), tr, t_si[qt - 1])
                u.free = [ta]
                t_si[qt - 1] = ta
        t_ct, t_ck = latent
        t_index = pe.last()
        for qt in range(1, 4):
            so = sidx[qt - 1]
            t_si[qt - 1] = dve.op(lambda e, so=so, qt=qt: e.tensor_tensor(
                so[:, qt * 128:qt * 128 + 128], so[:, qt * 128:qt * 128 + 128], cmask, ALU.add), t_si[qt - 1])
            dump(f"sidx{qt}", so[:, :])

        rounds = [r for r in range(16)]

        def topk_round():
            if not rounds:
                return
            rounds.pop(0)
            bs = [top8.next() for _ in range(3)]
            ts = [dve.op(lambda e, b=b, i=i: e.max(b.t[:, :], sidx[i][:, :]), t_si[i], *b.free)
                  for i, b in enumerate(bs)]
            for i, b in enumerate(bs):
                t_si[i] = dve.op(lambda e, b=b, i=i: e.match_replace(sidx[i][:, :], b.t[:, :], sidx[i][:, :], TAKEN),
                                 ts[i])
                b.free = [t_si[i]]

        Q.close()
        rt += [Buf(sb(R, f"rs{i}", [128, 515])) for i in range(4)]
        for r_ in rt[4:]:
            r_.free = [t_index]
        xrs, grs, b2s, b3s = rt[0::4], rt[1::4], rt[2::4], rt[3::4]
        xcs, y = tmp.bufs[0:2], tmp.bufs[2]
        t_pad = [pool.op(lambda e, r_=r_: e.memset(r_.t[:, 0:3], 0.0), *r_.free) for r_ in xrs]
        hg_ready = []
        pe.wait(t_rg)
        t_conv, t_part, t_sig = {}, {}, {}

        def branch_in(c):
            xr, xc = xrs[c % 2], xcs[c % 2]
            (bank,), (t,) = gemm(XH, XL, FULL, x2_ready)
            tx = act.op(lambda e: e.copy(xr.t[:, 3:515], bank.t[:, :]), t, *xr.free)
            bank.free = [tx]
            t = dve.op(lambda e: e.tensor_scalar(xc.t[:, 0:512], xr.t[:, 0:512], g("conv_w2", c * 4),
                                                 g("conv_b2", c), ALU.mult, ALU.add), tx, t_pad[c % 2], *xc.free)
            for k in range(1, 4):
                t = dve.op(lambda e, k=k: e.scalar_tensor_tensor(
                    xc.t[:, 0:512], xr.t[:, k:k + 512], g("conv_w2", c * 4 + k), xc.t[:, 0:512],
                    ALU.mult, ALU.add), t)
            xr.free = [t]
            t_conv[c] = t

        def branch_gates(c):
            xc, b2, b3 = xcs[c % 2], b2s[c % 2], b3s[c % 2]
            ba, bx = gemm_banks.next(), gemm_banks.next()
            ta = mm_group([(ba.t[:, :], rg[:, 0, c, :], xc.t[:, 0:512])], t_conv[c], *ba.free)
            tb = mm_group([(bx.t[:, :], rg[:, 1, c, :], xc.t[:, 0:512])], *bx.free)
            tr = act.op(lambda e: e.activation(b2.t[:, 0:512], ba.t[:, :], ACT.Sigmoid, bias=g("b_a", c)), ta,
                        *b2.free)
            ti = act.op(lambda e: e.activation(b3.t[:, 0:512], bx.t[:, :], ACT.Sigmoid, bias=g("b_x", c)), tb,
                        *b3.free)
            ba.free, bx.free = [tr], [ti]
            tix = dve.op(lambda e: e.tensor_tensor(xc.t[:, 0:512], b3.t[:, 0:512], xc.t[:, 0:512], ALU.mult), ti, tb)
            t_part[c] = (tr, tix)

        def branch_silu(c):
            gr_ = grs[c % 2]
            (bank,), (t,) = gemm(XH, XL, FULL, x2_ready)
            ts = act.op(lambda e: e.activation(gr_.t[:, 0:512], bank.t[:, :], ACT.Sigmoid), t, *gr_.free)
            ts = dve.op(lambda e: e.tensor_tensor(gr_.t[:, 0:512], gr_.t[:, 0:512], bank.t[:, :], ALU.mult), ts)
            bank.free = [ts]
            t_sig[c] = ts

        def merge_gate(m):
            (bank,), (t,) = gemm(XH, XL, FULL, x2_ready)
            ts = act.op(lambda e: e.activation(mixed[:, m, :], bank.t[:, :], ACT.Sigmoid, bias=g("b_merge", 8 + m)), t)
            bank.free = [ts]
            t_mg.append(ts)

        def branch_out(c):
            xc, b2, b3, gr_ = xcs[c % 2], b2s[c % 2], b3s[c % 2], grs[c % 2]
            tr, tix = t_part[c]
            tt1 = act.op(lambda e: e.activation(b3.t[:, 0:512], b2.t[:, 0:512], ACT.Tanh, scale=sps[:, 7, c:c + 1]),
                         tr, tix, t_sp)
            tt2 = act.op(lambda e: e.activation(b2.t[:, 0:512], b2.t[:, 0:512], ACT.Exp, scale=sps[:, 6, c:c + 1]),
                         tt1)
            t = dve.op(lambda e: e.tensor_tensor(y.t[:, 0:512], b2.t[:, 0:512], b2.t[:, 0:512], ALU.mult), tt2, *y.free)
            t = dve.op(lambda e: e.scalar_tensor_tensor(y.t[:, 0:512], y.t[:, 0:512], 1.0, b3.t[:, 0:512], ALU.add,
                                                        ALU.mult), t)
            t = act.op(lambda e: e.sqrt(y.t[:, 0:512], y.t[:, 0:512]), t)
            t = dve.op(lambda e: e.tensor_tensor(y.t[:, 0:512], y.t[:, 0:512], xc.t[:, 0:512], ALU.mult), t)
            xc.free = [t]
            t = dve.op(lambda e: e.tensor_tensor_scan(b3.t[:, 0:512], b2.t[:, 0:512], y.t[:, 0:512], 0.0,
                                                      ALU.mult, ALU.add), t)
            b2.free = y.free = [t]
            t = dve.op(lambda e: e.tensor_tensor(gr_.t[:, 0:512], gr_.t[:, 0:512], b3.t[:, 0:512], ALU.mult), t,
                       t_sig[c])
            b3.free = [t]
            parts_ = split(gr_.t[:, 0:512], t, hgh[:, c, :], hgl[:, c, :])
            gr_.free = list(parts_)
            hg_ready.append(parts_)

        t_mg = []
        branch_in(0)
        topk_round()
        topk_round()
        lam = gn[:, GCOL["lam"]:GCOL["lam"] + 8]
        dve.op(lambda e: e.tensor_scalar(sps[:, 0, :], lam, -1.0, 0.0, ALU.mult, ALU.max))
        t = act.op(lambda e: e.activation(sps[:, 1, :], lam, ACT.Abs))
        t = act.op(lambda e: e.activation(sps[:, 1, :], sps[:, 1, :], ACT.Exp, scale=-1.0), t)
        t = dve.op(lambda e: e.tensor_scalar(sps[:, 2, :], sps[:, 1, :], 1.0, None, ALU.add), t)
        tl = act.op(lambda e: e.activation(sps[:, 3, :], sps[:, 2, :], ACT.Ln), t)
        t = dve.op(lambda e: e.tensor_scalar(sps[:, 4, :], sps[:, 2, :], -1.0, None, ALU.add), t)
        t = dve.op(lambda e: e.tensor_scalar(sps[:, 5, :], sps[:, 4, :], 0.0, None, ALU.is_equal), t)
        t = dve.op(lambda e: e.tensor_tensor(sps[:, 4, :], sps[:, 4, :], sps[:, 5, :], ALU.add), t)
        t = dve.op(lambda e: e.reciprocal(sps[:, 4, :], sps[:, 4, :]), t)
        t = dve.op(lambda e: e.tensor_tensor(sps[:, 3, :], sps[:, 3, :], sps[:, 5, :], ALU.add), t, tl)
        t = dve.op(lambda e: e.tensor_tensor(sps[:, 4, :], sps[:, 4, :], sps[:, 3, :], ALU.mult), t)
        t = dve.op(lambda e: e.tensor_tensor(sps[:, 4, :], sps[:, 4, :], sps[:, 1, :], ALU.mult), t)
        t = dve.op(lambda e: e.tensor_tensor(sps[:, 4, :], sps[:, 4, :], sps[:, 0, :], ALU.add), t)
        t = dve.op(lambda e: e.tensor_scalar(sps[:, 6, :], sps[:, 4, :], -8.0, None, ALU.mult), t)
        t_sp = dve.op(lambda e: e.tensor_scalar(sps[:, 7, :], sps[:, 4, :], 8.0, None, ALU.mult), t)

        for c in range(8):
            if c + 1 < 8:
                branch_in(c + 1)
            branch_gates(c)
            branch_silu(c)
            if c < 5:
                merge_gate(c)
            branch_out(c)
            if c < 6:
                topk_round()
        for m in range(5, 8):
            merge_gate(m)

        for m in range(8):
            (by,), (ty,) = gemm(hgh, hgl, FULL, hg_ready)
            t_mix = dve.op(lambda e, m=m, by=by: e.tensor_tensor(mixed[:, m, :], by.t[:, :], mixed[:, m, :],
                                                                 ALU.mult), t_mg[m], ty)
            by.free = [t_mix]
            topk_round()
        dump("mixed", mixed[:, :, :])
        t_dt = [None]
        for qt in range(1, 4):
            n = 128 * (qt + 1)
            so, do = sidx[qt - 1], dt_[qt - 1]
            t = dve.op(lambda e, so=so, n=n: e.tensor_scalar(so[:, :], so[:, :], TAKEN, -1.0, ALU.is_equal, ALU.add),
                       t_si[qt - 1])
            t_dt.append(dve.op(lambda e, so=so, do=do, qt=qt: e.scalar_tensor_tensor(
                do[:, :], so[:, :], BIG, dist[:, 384 - 128 * qt:512], ALU.mult, ALU.add), t))

        fence()
        R.close()

        G = ExitStack()
        qT = sb(G, "qT", [128, 8, 512])
        qlr = Ring([Buf(sb(G, f"ql{i}", [128, 512])) for i in range(2)])
        ga = sb(G, "ga", [128, 8, 512])
        ma = sb(G, "ma", [128, 8, 512])
        uk = sb(G, "uk", [128, 8, 128])
        t_uk = c_e[2].start(sp, uk[:, :, :], w_uk)
        for m in range(8):
            (bank,), (t,) = gemm(XH, XL, FULL, x2_ready)
            t_q = act.op(lambda e, m=m, bank=bank: e.copy(qT[:, m, :], bank.t[:, :]), t)
            bank.free = [t_q]
        for m in range(8):
            (bank,), (t,) = gemm(XH, XL, FULL, x2_ready)
            te = act.op(lambda e, m=m, bank=bank: e.activation(ga[:, m, :], bank.t[:, :], ACT.Silu), t)
            bank.free = [te]
        t_ga = te
        for m in range(8):
            (bank,), (t,) = gemm(XH, XL, FULL, x2_ready)
            te = act.op(lambda e, m=m, bank=bank: e.activation(ma[:, m, :], bank.t[:, :], ACT.Sigmoid,
                                                               bias=g("b_merge", m)), t)
            bank.free = [te]
        t_ma = te
        x_used = pe.last()

        fence()
        wide_p = [Buf(rb[:, :]), Buf(diag[:, :, :].rearrange("p j c -> p (j c)"))]
        Pb = Ring(sq.bufs + [Buf(sb(G, f"eP{i}", [128, 512])) for i in range(2)] + wide_p)
        PTb = Ring([Buf(sb(G, f"ePT{i}", [128, 512])) for i in range(3)])
        mx = Ring([Buf(sb(G, f"emx{i}", [128, 4])) for i in range(6)])
        og_ready = [None] * 8
        halves = [Buf(wide[i // 2].t[:, 512 * (i % 2):512 * (i % 2) + 512]) for i in range(4)]
        s_banks = Ring([Buf(b.t[:, :]) for b in banks[0:2]])
        t_banks = Ring(halves[0:2])
        q_bank, o_banks = halves[2], [halves[3], Buf(banks[2].t[:, :])]
        pair = Buf(banks[3].t[:, :])
        q_of, unit, o_of = {}, {}, {}

        def latent_q(hd):
            ql = qlr.next()
            b0 = 64 * (hd % 2)
            t = mm_group([(q_bank.t, uk[b0:b0 + 64, hd // 2, :], qT[b0:b0 + 64, hd // 2, :])], t_q, t_uk,
                         *q_bank.free)
            t = act.op(lambda e: e.mul(ql.t[:, :], q_bank.t, 0.125), t, *ql.free)
            q_bank.free = [t]
            q_of[hd] = (ql, t)

        def scores2(hd, qt):
            n = 128 * (qt + 1)
            ql, t_ql = q_of[hd]
            bank = s_banks.next()
            tS = mm_group([(bank.t[:, 0:n], ql.t[:, qt * 128:qt * 128 + 128], ckvT[:, 0:n])], t_ql, t_ct, *bank.free)
            if qt == 3:
                ql.free = [tS]
            unit[hd, qt] = (bank, tS)

        def soften2(hd, qt):
            slope = float(np.exp2(np.float32(-8.0 * (hd + 1) / 16)))
            n = 128 * (qt + 1)
            bank, tS = unit[hd, qt]
            P, m = Pb.next(), mx.next()
            dd = dist[:, 384:512] if qt == 0 else dt_[qt - 1][:, :]
            t5 = dve.op(lambda e: e.scalar_tensor_tensor(P.t[:, 0:n], dd, slope, bank.t[:, 0:n], ALU.mult, ALU.add),
                        tS, t_dt[qt], *P.free)
            bank.free = [t5]
            t6 = dve.op(lambda e: e.tensor_reduce(m.t[:, 0:1], P.t[:, 0:n], AX.X, ALU.max, negate=True), t5, *m.free)
            t7 = act.op(lambda e: e.activation(P.t[:, 0:n], P.t[:, 0:n], ACT.Exp, bias=m.t[:, 0:1],
                                               accum_out=m.t[:, 1:2]), t6)
            unit[hd, qt] = (P, m, t7)

        def normalize2(hd, qt):
            P, m, t7 = unit[hd, qt]
            n = 128 * (qt + 1)
            t8 = dve.op(lambda e: e.reciprocal(m.t[:, 2:3], m.t[:, 1:2]), t7)
            t9 = dve.op(lambda e: e.tensor_scalar(P.t[:, 0:n], P.t[:, 0:n], m.t[:, 2:3], None, ALU.mult), t8)
            m.free = [t9]
            unit[hd, qt] = (P, t9)

        def turn2(hd, qt):
            P, t9 = unit[hd, qt]
            pt, wb = PTb.next(), t_banks.next()
            pe.wait(t9, *wb.free)
            for i in range(qt + 1):
                f = lambda e, i=i: e.transpose(wb.t[:, i * 128:i * 128 + 128], P.t[:, i * 128:i * 128 + 128], ident)
                if i < qt:
                    pe.silent(f)
            tT = pe.op(f)
            P.free = [tT]
            t = act.op(lambda e: e.copy(pt.t[:, 0:128 * (qt + 1)], wb.t[:, 0:128 * (qt + 1)]), tT, *pt.free)
            wb.free = [t]
            unit[hd, qt] = (pt, t)

        def values2(hd, qt):
            pt, t = unit.pop((hd, qt))
            o_bank = o_banks[hd % 2]
            pe.wait(t, t_ck)
            if qt == 0:
                pe.wait(*o_bank.free)
            o = o_bank.t[:, qt * 128:qt * 128 + 128]
            for i in range(qt + 1):
                f = lambda e, i=i: e.matmul(o, ckv[:, i, :], pt.t[:, i * 128:i * 128 + 128], start=(i == 0),
                                            stop=(i == qt), skip_group_check=True)
                if i < qt:
                    pe.silent(f)
            tO = pe.op(f)
            pt.free = [tO]
            if qt == 3:
                ol = tmp.next()
                te = act.op(lambda e: e.copy(ol.t[:, 0:512], o_bank.t), tO, *ol.free)
                o_bank.free = [te]
                o_of[hd] = (ol, te)

        def out_head(hd):
            ol, te = o_of.pop(hd)
            b0 = 64 * (hd % 2)
            if hd % 2 == 0:
                pe.wait(*pair.free)
            tO = pe.op(lambda e: e.matmul(pair.t[b0:b0 + 64, :], uv[:, hd, :], ol.t[:, 0:512], start=True, stop=True,
                                          skip_group_check=True), te, t_uv)
            ol.free = [tO]
            if hd % 2 == 1:
                c = hd // 2
                u = tmp.next()
                t = dve.op(lambda e: e.tensor_tensor(u.t[:, 0:512], pair.t, ga[:, c, :], ALU.mult), tO, t_ga, *u.free)
                pair.free = [t]
                r_ = split(u.t[:, 0:512], t, XH[:, c, 0:512], XL[:, c, 0:512], x_used)
                u.free = list(r_)
                og_ready[c] = r_

        units = [(hd, qt) for hd in range(16) for qt in range(4)]
        latent_q(0)
        for n in range(len(units) + 7):
            if n < len(units):
                scores2(*units[n])
            if 0 <= n - 3 < len(units):
                turn2(*units[n - 3])
            if n < len(units):
                soften2(*units[n])
                if units[n][1] == 1 and units[n][0] + 1 < 16:
                    latent_q(units[n][0] + 1)
            if 0 <= n - 1 < len(units):
                normalize2(*units[n - 1])
            if 0 <= n - 4 < len(units):
                values2(*units[n - 4])
            if 0 <= n - 6 < len(units) and units[n - 6][1] == 3:
                out_head(units[n - 6][0])
        (rb_free[0],), (diag_free[0],) = wide_p[0].free, wide_p[1].free
        for b, v in zip(banks, s_banks.bufs + [o_banks[1], pair]):
            b.free = v.free
        for i in range(2):
            wide[i].free = halves[2 * i].free + halves[2 * i + 1].free
        t_mx = []
        for m in range(8):
            (bank,), (t,) = gemm(XH, XL, FULL, og_ready)
            u = tmp.next()
            t1 = dve.op(lambda e, m=m, u=u, bank=bank: e.tensor_tensor(u.t[:, 0:512], bank.t[:, :], ma[:, m, :], ALU.mult),
                        t, t_ma, *u.free)
            bank.free = [t1]
            t2 = dve.op(lambda e, m=m, u=u: e.tensor_tensor(mixed[:, m, :], u.t[:, 0:512], mixed[:, m, :], ALU.add),
                        t1, t_mix)
            u.free = [t2]
            t_mx.append(t2)
        last_y = pe.last()
        mix_ready = [split(mixed[:, m, :], t_mx[m], XH[:, m, 0:512], XL[:, m, 0:512], last_y,
                           lo=pool if m % 3 == 1 else dve) for m in range(8)]
        nl = Norm(512, wide[0], acc=tmp.next())
        for m in range(8):
            (bank,), (t,) = gemm(XH, XL, FULL, mix_ready)
            if m > 0:
                nl.add(hx[m - 1], t_hk[m - 1])
            if m == 7:
                warm_sqrt()
            tt = dve.op(lambda e, m=m, bank=bank: e.tensor_tensor(hx[m], bank.t[:, :], hx[m], ALU.add), t)
            bank.free = [tt]
            t_hk[m] = tt
        nl.add(hx[7], t_hk[7], last=True)
        t_bc = spread(nl.tts, nl.scale(D), 2, wide[1], to_psum=True)
        c_out = channel("c_out")
        for k in range(KT):
            t = dve.op(lambda e, k=k: e.scalar_tensor_tensor(hx[k], hx[k], g("g_fin2", k), wide[1].t[:, 0:512],
                                                             ALU.mult, ALU.mult), t_bc)
            t_out = c_out.start(sp, out[:, k, :], hx[k], t)
        sp.wait(t_out)
        G.close()
        E.close()

        block = ctx.enter_context(nc.Block())

        def run(engine):
            def body(e):
                for f in engine.queue:
                    f(e)
            return body

        block.tensor(run(pe))
        block.vector(run(dve))
        block.scalar(run(act))
        block.gpsimd(run(pool))
        block.sync(run(sp))


def _tiles(w):
    k, m = w.shape
    return w.reshape(k // 128, 128, m // 128, 128).transpose(2, 1, 0, 3).reshape(m // 128, 128, k)


def _cols(v):
    return v.reshape(-1, 128).T


def _constants():
    p = np.arange(128)[:, None]
    q = np.arange(128)[None, :]
    x = np.arange(512)[None, :]
    c = np.zeros((128, 1024), np.float32)
    c[:, 0:128] = p == q
    c[:, 128:256] = np.where(q <= p, 0.0, -BIG)
    c[:, 256:384] = q
    c[:, 384:896] = np.where(x - 384 - p <= 0, x - 384 - p, -BIG)
    c[:, 896:1024] = 1.0
    t = np.zeros((128, T), np.float32)
    freqs = np.float32(10000.0) ** (-np.arange(16, dtype=np.float32) / np.float32(16))
    ang = np.arange(T, dtype=np.float32)[:, None] * freqs[None, :].astype(np.float32)
    cos, sin = np.cos(ang).T, np.sin(ang).T
    t[64:80] = t[80:96] = cos
    t[96:112] = -sin
    t[112:128] = sin
    return c, t


def layouts(a):
    f = np.float32
    zeros = lambda *s: np.zeros(s, f)
    hT = np.concatenate([a["meta"], a["x"][0]], 0).T.reshape(8, 128, T).transpose(1, 0, 2)
    w_in = a["w_in"][0]
    r = w_in[:, 1408:1440]
    rope = np.concatenate([zeros(D, 64), r, r[:, 16:], r[:, :16]], 1)
    first = [w_in[:, 1024:1280], w_in[:, 1280:1408], rope]
    for c in range(4):
        first += [w_in[:, c * 128:c * 128 + 128], w_in[:, 512 + c * 128:640 + c * 128]]
    wo = _tiles(a["w_out"][0]).reshape(4, 2, 128, 2, 512).transpose(3, 0, 2, 1, 4).reshape(8, 128, 1024)
    parts = [_tiles(np.concatenate(first, 1)), wo, _tiles(a["peer_wq"][0])]
    U = a["peer_u"][0].reshape(128, 128, 8, 128).transpose(0, 3, 2, 1).reshape(16, 8, 128, 1024)
    V = a["peer_v"][0].reshape(16, 8, 128, 8, 128).transpose(0, 3, 2, 1, 4).reshape(16, 8, 128, 1024)
    parts += [U[i] for i in range(SPILLED)]
    for what, n, i in expert_steps():
        if what == "V" or ORDER[n] >= SPILLED:
            parts.append((V if what == "V" else U)[ORDER[n]][i:i + 1])
    w2 = a["w_in_2"][0]
    o = np.cumsum([0, 1024, 128, 512, 64, 8, 1024, 1024, 1024, 2048])
    q, ckv, qi, ki, wi, ga, xr, gr, mg = [w2[:, o[i]:o[i + 1]] for i in range(9)]
    parts.append(_tiles(np.concatenate([ki, wi, zeros(D, 56), qi, ckv], 1)))
    xr, gr, mg, rp = _tiles(xr), _tiles(gr), _tiles(mg), _tiles(a["w_rnn_proj_2"][0])
    parts.append(xr[0:1])
    for c in range(8):
        parts += [xr[c + 1:c + 2], gr[c:c + 1]] + ([mg[8 + c:9 + c]] if c < 5 else [])
    parts += [mg[13:16], rp]
    parts += [_tiles(q), _tiles(ga), mg[:8], _tiles(a["w_attn_proj_2"][0]), _tiles(a["w_out_2"][0])]
    wstream = np.concatenate(parts, 0)

    uq = a["w_uq"][0].reshape(2, 128, 8, 96)
    uq = np.concatenate([uq, uq[..., 80:96], uq[..., 64:80]], -1).transpose(1, 2, 0, 3).reshape(128, 2048)
    keys = a["peer_keys"][0].transpose(1, 3, 0, 2).reshape(128, 8, 128)
    uk = a["w_uk_2"][0].reshape(8, 2, 128, 64).transpose(1, 3, 0, 2).reshape(128, 8, 128)
    uv = a["w_uv_2"][0].transpose(1, 0, 2)
    rg = zeros(128, 2, 8, 128)
    for i, n in enumerate(("w_rg_a_2", "w_rg_x_2")):
        w = a[n][0].reshape(8, 2, 64, 64).transpose(1, 2, 0, 3)
        rg[0:64, i, :, 0:64] = w[0]
        rg[64:128, i, :, 64:128] = w[1]
    pad64 = lambda v: np.concatenate([v, zeros(64)])
    gv = {
        "g_mix": a["g_mix_norm"][0], "g_q": a["g_q"][0], "g_kv": a["g_kv"][0], "conv_b": a["conv_b"][0],
        "g_ln": a["g_conv_ln"][0], "b_ln": a["b_conv_ln"][0], "g_oa": a["g_out_attn"][0],
        "g_oc": a["g_out_conv"][0], "g_ffn": a["g_ffn_norm"][0], "g_fin": a["g_final"],
        "g2": a["norm_gain_2"][0], "b_merge": a["b_merge_2"][0], "g_kv2": a["kv_norm_gain_2"][0],
        "g_idx": pad64(a["idx_ln_gain_2"][0]), "b_idx": pad64(a["idx_ln_bias_2"][0]),
        "conv_b2": a["conv_b_2"][0], "b_a": a["b_rg_a_2"][0], "b_x": a["b_rg_x_2"][0],
        "lam": a["lru_lambda_2"][0], "g_fin2": a["final_norm_gain_2"],
    }
    cols = []
    for name, n in GAINS:
        if name == "conv_w":
            cols.append(a["conv_w"][0].reshape(31, 4, 128).transpose(2, 1, 0).reshape(128, 124))
        elif name == "conv_w2":
            cols.append(a["conv_w_2"][0].reshape(4, 8, 128).transpose(2, 1, 0).reshape(128, 32))
        else:
            cols.append(_cols(gv[name]))
    c, t = _constants()
    return {
        "hT": hT, "wstream": wstream, "gains": np.concatenate(cols, 1), "consts": c, "trig": t, "w_uq": uq,
        "w_ukv": a["w_ukv"][0], "keys": keys, "w_uk": uk, "w_uv": uv, "w_rg": rg,
    }


def kernel(**inputs):
    import concourse.bacc as _bacc
    from concourse.bass_utils import run_bass_kernel_spmd as _run

    a = {k: np.asarray(v) for k, v in inputs.items()}
    arrays = {k: np.ascontiguousarray(v) for k, v in layouts(a).items()}
    nc = _bacc.Bacc("TRN2", target_bir_lowering=False, num_devices=1)
    args = {k: nc.dram_tensor(f"in_{k}", v.shape, F32, kind="ExternalInput").ap() for k, v in arrays.items()}
    out = nc.dram_tensor("out_0", (128, 8, 512), F32, kind="ExternalOutput").ap()
    build_program(nc, out=out, **args)
    r = _run(nc, [{f"in_{k}": v for k, v in arrays.items()}], core_ids=[0])
    y = np.asarray(r.results[0]["out_0"])
    return np.ascontiguousarray(y.transpose(1, 0, 2).reshape(1024, 512).T)[None]
```
